# Optimizing a Trainium2 kernel written in Bass

```python
import jax, jax.numpy as jnp
from jax import lax
import numpy as np

D_MODEL = 1024
BATCH = 1
SEQ = 1024
DEPTH = 1

CHUNK = 64
LN_EPS = 1e-5
DEEPNORM_ALPHA = (2 * DEPTH) ** 0.25
DEEPNORM_BETA = (8 * DEPTH) ** -0.25

GLA_HEADS = 4
GLA_DK = D_MODEL // 2
GLA_DV = D_MODEL
GLA_HK = GLA_DK // GLA_HEADS
GLA_HV = GLA_DV // GLA_HEADS
GLA_RANK = 16
GLA_TAU = 16.0

SWA_HEADS = 16
SWA_KV_HEADS = 4
SWA_GROUP = SWA_HEADS // SWA_KV_HEADS
SWA_HD = 64
SWA_WINDOW = 128
SWA_NBAND = -(-SWA_WINDOW // CHUNK)
SWA_BAND = SWA_NBAND * CHUNK
NEG_INF = -1e30

REL_BUCKETS = 32
REL_MAX_DIST = 128

N_GROUPS = 4
EXPERTS_PER_GROUP = 8
N_EXPERTS = N_GROUPS * EXPERTS_PER_GROUP
TOP_K = 2
D_EXPERT = 512
MOE_BLOCK = 128

PLE_DIM = 256

IN_SPLITS = (GLA_DK, GLA_DK, GLA_DV, GLA_RANK, GLA_DV,
             SWA_HEADS * SWA_HD, SWA_KV_HEADS * SWA_HD, SWA_KV_HEADS * SWA_HD,
             D_MODEL, D_MODEL)
IN_WIDTH = sum(IN_SPLITS)

kernel_name = "hybrid_gla_swa_hmoe_block"

def layer_norm(x, g, b):
    xf = x.astype(jnp.float32)
    mu = jnp.mean(xf, -1, keepdims=True)
    var = jnp.mean(jnp.square(xf - mu), -1, keepdims=True)
    y = (xf - mu) * lax.rsqrt(var + LN_EPS) * g.astype(jnp.float32) + b.astype(jnp.float32)
    return y.astype(x.dtype)

def gla_mixer(q, k, v, gate_lr, r, w_gate_up, b_gate, norm_g):
    B, T, _ = q.shape
    NC = T // CHUNK
    f32 = jnp.float32
    qh = q.astype(f32).reshape(B, NC, CHUNK, GLA_HEADS, GLA_HK) * (GLA_HK ** -0.5)
    kh = k.astype(f32).reshape(B, NC, CHUNK, GLA_HEADS, GLA_HK)
    vh = v.astype(f32).reshape(B, NC, CHUNK, GLA_HEADS, GLA_HV)
    log_a = jax.nn.log_sigmoid((gate_lr @ w_gate_up + b_gate).astype(f32)) / GLA_TAU
    log_a = log_a.reshape(B, NC, CHUNK, GLA_HEADS, GLA_HK)
    cum = jnp.cumsum(log_a, axis=2)
    total = cum[:, :, -1]
    k_dec = kh * jnp.exp(total[:, :, None] - cum)
    gamma = jnp.exp(total)
    q_dec = qh * gamma[:, :, None]
    att = jnp.einsum('bnqhd,bnshd->bnhqs', qh, k_dec)
    o_intra = jnp.einsum('bnhqs,bnshe->bnqhe', att, vh)

    def step(S, inp):
        qd, kd, vc, g = inp
        o = jnp.einsum('bqhd,bhde->bqhe', qd, S)
        S = S * g[..., None] + jnp.einsum('bshd,bshe->bhde', kd, vc)
        return S, o

    S0 = jnp.zeros((B, GLA_HEADS, GLA_HK, GLA_HV), f32)
    xs = (jnp.moveaxis(q_dec, 1, 0), jnp.moveaxis(k_dec, 1, 0),
          jnp.moveaxis(vh, 1, 0), jnp.moveaxis(gamma, 1, 0))
    _, o_inter = lax.scan(step, S0, xs)
    o = (o_intra + jnp.moveaxis(o_inter, 0, 1)).reshape(B, T, GLA_HEADS, GLA_HV)
    o = o * lax.rsqrt(jnp.mean(jnp.square(o), -1, keepdims=True) + LN_EPS)
    o = o * norm_g.astype(f32).reshape(GLA_HEADS, GLA_HV)
    o = o.reshape(B, T, GLA_DV) * jax.nn.silu(r.astype(f32))
    return o.astype(q.dtype)

def t5_bucket(rel):
    nb = REL_BUCKETS // 2
    ret = (rel > 0).astype(np.int32) * nb
    n = np.abs(rel)
    max_exact = nb // 2
    large = max_exact + (np.log(np.maximum(n, 1) / max_exact)
                         / np.log(REL_MAX_DIST / max_exact) * (nb - max_exact)).astype(np.int32)
    large = np.minimum(large, nb - 1)
    return ret + np.where(n < max_exact, n, large)

def swa_rel_bias(rel_table):
    q_pos = (SWA_NBAND - 1) * CHUNK + np.arange(CHUNK)
    k_pos = np.arange(SWA_BAND)
    buckets = t5_bucket(k_pos[None, :] - q_pos[:, None])
    bias = rel_table.astype(jnp.float32)[buckets]
    return jnp.transpose(bias, (2, 0, 1)).reshape(SWA_KV_HEADS, SWA_GROUP, 1, CHUNK, SWA_BAND)

def swa_mixer(q, k, v, sinks, rel_table):
    B, T, _ = q.shape
    NC = T // CHUNK
    f32 = jnp.float32
    qh = q.astype(f32).reshape(B, NC, CHUNK, SWA_KV_HEADS, SWA_GROUP, SWA_HD) * (SWA_HD ** -0.5)
    kh = k.astype(f32).reshape(B, NC, CHUNK, SWA_KV_HEADS, SWA_HD)
    vh = v.astype(f32).reshape(B, NC, CHUNK, SWA_KV_HEADS, SWA_HD)
    pad = ((0, 0), (SWA_NBAND - 1, 0), (0, 0), (0, 0), (0, 0))
    kp = jnp.pad(kh, pad)
    vp = jnp.pad(vh, pad)
    kb = jnp.concatenate([kp[:, j:j + NC] for j in range(SWA_NBAND)], axis=2)
    vb = jnp.concatenate([vp[:, j:j + NC] for j in range(SWA_NBAND)], axis=2)
    s = jnp.einsum('bnqhgd,bnkhd->bhgnqk', qh, kb) + swa_rel_bias(rel_table)
    key_chunk = np.arange(NC)[:, None] + (np.arange(SWA_BAND) // CHUNK)[None, :] - (SWA_NBAND - 1)
    valid = jnp.asarray(key_chunk >= 0)[:, None, :]
    s = jnp.where(valid, s, NEG_INF)
    sink = sinks.astype(f32).reshape(SWA_KV_HEADS, SWA_GROUP, 1, 1, 1)
    m = jnp.maximum(jnp.max(s, -1, keepdims=True), sink)
    e = jnp.exp(s - m)
    probs = e / (jnp.sum(e, -1, keepdims=True) + jnp.exp(sink - m))
    o = jnp.einsum('bhgnqk,bnkhd->bnqhgd', probs, vb).reshape(B, T, SWA_HEADS * SWA_HD)
    return o.astype(q.dtype)

def hier_moe(x, w_group, b_group, w_exp_router, b_exp_router, w_gate, w_up, w_down):
    B, T, D = x.shape
    N = B * T
    f32 = jnp.float32
    xt = x.reshape(N, D)
    glog = (xt @ w_group + b_group).astype(f32)
    gprob = jax.nn.softmax(glog, -1)
    _, grp = lax.top_k(glog, 1)
    pg = jnp.take_along_axis(gprob, grp, -1)[:, 0]
    elog = (jnp.einsum('nd,gde->nge', xt, w_exp_router) + b_exp_router).astype(f32)
    elog_sel = jnp.take_along_axis(elog, grp[:, :, None], axis=1)[:, 0]
    top_v, top_i = lax.top_k(elog_sel, TOP_K)
    wk = jax.nn.softmax(top_v, -1) * pg[:, None]
    expert = grp * EXPERTS_PER_GROUP + top_i

    A = N * TOP_K
    e_flat = expert.reshape(A)
    tok_flat = jnp.repeat(jnp.arange(N, dtype=jnp.int32), TOP_K)
    w_flat = wk.reshape(A)
    order = jnp.argsort(e_flat)
    e_s, tok_s, w_s = e_flat[order], tok_flat[order], w_flat[order]
    counts = jax.ops.segment_sum(jnp.ones((A,), jnp.int32), e_flat, num_segments=N_EXPERTS)
    starts = jnp.cumsum(counts) - counts
    padded = (counts + MOE_BLOCK - 1) // MOE_BLOCK * MOE_BLOCK
    pend = jnp.cumsum(padded)
    pstart = pend - padded
    dest = pstart[e_s] + (jnp.arange(A, dtype=jnp.int32) - starts[e_s])
    P = A + N_EXPERTS * MOE_BLOCK
    NB = P // MOE_BLOCK
    slot_tok = jnp.zeros((P,), jnp.int32).at[dest].set(tok_s)
    slot_w = jnp.zeros((P,), f32).at[dest].set(w_s)
    block_e = jnp.clip(jnp.searchsorted(pend, jnp.arange(NB) * MOE_BLOCK, side='right'),
                       0, N_EXPERTS - 1)
    xb = xt[slot_tok].reshape(NB, MOE_BLOCK, D)

    def run_block(args):
        xblk, e = args
        h = jax.nn.silu(xblk @ w_gate[e]) * (xblk @ w_up[e])
        return h @ w_down[e]

    yb = lax.map(run_block, (xb, block_e)).reshape(P, D)
    y = jax.ops.segment_sum(yb * slot_w[:, None].astype(yb.dtype), slot_tok, num_segments=N)
    return y.reshape(B, T, D)

def setup_inputs(seed: int = 0) -> dict:
    key = jax.random.key(seed)
    ks = iter(jax.random.split(key, 48))
    L, D = DEPTH, D_MODEL
    beta = DEEPNORM_BETA

    def nrm(shape, scale):
        return jax.random.normal(next(ks), shape, jnp.float32) * scale

    in_scales = (1.0, 1.0, beta, 1.0, 1.0, 1.0, 1.0, beta, 1.0, 1.0)
    w_in = jnp.concatenate([nrm((L, D, w), D ** -0.5 * s) for w, s in zip(IN_SPLITS, in_scales)], -1)
    return {
        "x": nrm((BATCH, SEQ, D), 1.0),
        "p": nrm((L, BATCH, SEQ, PLE_DIM), 1.0),
        "rel_table": nrm((REL_BUCKETS, SWA_HEADS), 0.5),
        "w_in": w_in,
        "gla_gate_up": nrm((L, GLA_RANK, GLA_DK), GLA_RANK ** -0.5),
        "gla_gate_b": nrm((L, GLA_DK), 0.1),
        "gla_norm_g": 1.0 + nrm((L, GLA_DV), 0.02),
        "swa_sinks": nrm((L, SWA_HEADS), 0.5),
        "branch_gate_b": nrm((L, 2, D), 0.02),
        "w_branch_gla": nrm((L, GLA_DV, D), beta * GLA_DV ** -0.5),
        "w_branch_swa": nrm((L, SWA_HEADS * SWA_HD, D), beta * (SWA_HEADS * SWA_HD) ** -0.5),
        "w_out": nrm((L, D, D), beta * D ** -0.5),
        "ln1_g": 1.0 + nrm((L, D), 0.02),
        "ln1_b": nrm((L, D), 0.02),
        "router_group_w": nrm((L, D, N_GROUPS), D ** -0.5),
        "router_group_b": nrm((L, N_GROUPS), 0.01),
        "router_expert_w": nrm((L, N_GROUPS, D, EXPERTS_PER_GROUP), D ** -0.5),
        "router_expert_b": nrm((L, N_GROUPS, EXPERTS_PER_GROUP), 0.01),
        "expert_w_gate": nrm((L, N_EXPERTS, D, D_EXPERT), D ** -0.5),
        "expert_w_up": nrm((L, N_EXPERTS, D, D_EXPERT), D ** -0.5),
        "expert_w_down": nrm((L, N_EXPERTS, D_EXPERT, D), beta * D_EXPERT ** -0.5),
        "w_ple": nrm((L, PLE_DIM, D), beta * PLE_DIM ** -0.5),
        "w_ple_gate": nrm((L, D, D), D ** -0.5),
        "ple_gate_b": nrm((L, D), 0.02),
        "ln2_g": 1.0 + nrm((L, D), 0.02),
        "ln2_b": nrm((L, D), 0.02),
    }

def reference(x, p, rel_table, w_in, gla_gate_up, gla_gate_b, gla_norm_g, swa_sinks,
              branch_gate_b, w_branch_gla, w_branch_swa, w_out, ln1_g, ln1_b,
              router_group_w, router_group_b, router_expert_w, router_expert_b,
              expert_w_gate, expert_w_up, expert_w_down, w_ple, w_ple_gate, ple_gate_b,
              ln2_g, ln2_b):
    offs = [int(o) for o in np.cumsum((0,) + IN_SPLITS)]
    for i in range(DEPTH):
        z = x @ w_in[i]
        gq, gk, gv, glr, gr, sq, sk, sv, ga, gb = [z[..., offs[j]:offs[j + 1]]
                                                   for j in range(len(IN_SPLITS))]
        a = gla_mixer(gq, gk, gv, glr, gr, gla_gate_up[i], gla_gate_b[i], gla_norm_g[i])
        b = swa_mixer(sq, sk, sv, swa_sinks[i], rel_table)
        gate_a = jax.nn.sigmoid(ga + branch_gate_b[i, 0])
        gate_b = jax.nn.sigmoid(gb + branch_gate_b[i, 1])
        merged = gate_a * (a @ w_branch_gla[i]) + gate_b * (b @ w_branch_swa[i])
        x1 = layer_norm(DEEPNORM_ALPHA * x + merged @ w_out[i], ln1_g[i], ln1_b[i])
        y = hier_moe(x1, router_group_w[i], router_group_b[i], router_expert_w[i],
                     router_expert_b[i], expert_w_gate[i], expert_w_up[i], expert_w_down[i])
        ple = (p[i] @ w_ple[i]) * jax.nn.sigmoid(x1 @ w_ple_gate[i] + ple_gate_b[i])
        x = layer_norm(DEEPNORM_ALPHA * x1 + y + ple, ln2_g[i], ln2_b[i])
    return x


_drawn_inputs = setup_inputs


def setup_inputs(seed=0):
    import zlib

    import numpy as np

    out = dict(_drawn_inputs(seed))
    spreads = {}
    factors = {'rel_table': 6.403,
     'gla_gate_up': 4.271,
     'gla_gate_b': 7.235,
     'gla_norm_g': 27.264,
     'swa_sinks': 64.0,
     'branch_gate_b': 8.0,
     'w_branch_swa': 2.73,
     'router_group_b': 28.627,
     'router_expert_b': 8.0,
     'ple_gate_b': 27.351,
     'ln2_g': 8.039,
     'ln2_b': 8.084}
    for name, (base, spread) in spreads.items():
        noise = np.random.default_rng([zlib.crc32(name.encode()), seed]).standard_normal(out[name].shape)
        drawn = base * np.exp(spread * noise) if base else spread * noise
        out[name] = __import__('jax').numpy.asarray(drawn.astype(out[name].dtype))
    for name, factor in factors.items():
        out[name] = (out[name] * factor).astype(out[name].dtype)
    return out
```

```python
from contextlib import ExitStack, contextmanager

import numpy as np

import concourse.bass as bass
from concourse import mybir
from concourse.alu_op_type import AluOpType as ALU

ACT = mybir.ActivationFunctionType
AX = mybir.AxisListType
F32 = mybir.dt.float32
F32R = mybir.dt.float32r
I32 = mybir.dt.int32

P = 128
D = 1024
SEQ = 1024
NT = SEQ // P
KC = D // P
CHUNK = 64
ALPHA = 2.0 ** 0.25
EPS = 1e-5
SL = 512
NS = D // SL
CPS = SL // P
WC = KC // 2

GH, GK, GV, RANK, TAU = 4, 128, 256, 16, 16.0
HEADS, KVH, HD = 16, 4, 64
PAIRS = HEADS // 2
REL = 191
NEG = -1e30

NG, EPG, NE = 4, 8, 32
DE = 512
FC = DE // P
MAXB = 48
MINB = 16
RING = 5
NLOG = NG + NE
PLE = 256
PKC = PLE // P

C_GQ, C_GK, C_LR, C_R, C_SQ, C_SK, C_GA = 0, 512, 2048, 2064, 3088, 4112, 4624

S_SQ, S_SKV, S_GATE, S_GQ, S_LR, S_KV, S_R, S_WG, S_WS, S_WO, S_RT, S_PG, S_END = (
    0, 2, 3, 7, 8, 9, 12, 14, 16, 18, 20, 21, 23)
B_SQ, B_SK, B_SV, B_GATE, B_GQ, B_LR, B_KV, B_R, B_WG, B_WS, B_WO, B_RT, B_PG = (
    0, 8, 10, 14, 30, 34, 35, 47, 55, 63, 71, 79, 80)
Z_SQ, Z_GATE, Z_GQ, Z_ALL = 0, 8, 24, 28
E_SQ, E_SV, E_GATE, E_GQ, E_LR, E_KV = 0, 8, 12, 28, 32, 33

K_ID, K_SUF, K_ERL, K_ONE, K_CH, K_I8, K_I48, K_ALL = 0, 128, 256, 384, 512, 514, 522, 570
ARENA = 24900
CONSTS = 6 * 16
TL_X = 2 + 2 * NT
TL_A = TL_X + 2 * NT
TL_B = TL_A + KC
TL_M = TL_B + KC
TL_X1 = TL_M + 2 * NT


class Steps:

    def __init__(self):
        self.total, self.at = 0, 0
        self.i = self.per = None

    @contextmanager
    def loop(self, engine, n, per):
        with engine.Fori(0, n) as i:
            self.i, self.per, self.at = i, per, 0
            yield i
        assert self.at == per, (self.at, per)
        self.total += n * per
        self.i = None

    def done(self):
        if self.i is None:
            self.total += 1
            return self.total
        self.at += 1
        return self.i * self.per + (self.total + self.at)


def build(nc, a):
    ctx = ExitStack()
    with ctx:
        def dram(name, shape, dt=F32):
            return nc.dram_tensor(name, shape, dt, kind="Internal").ap()

        def sem(name):
            return ctx.enter_context(nc.semaphore(name))

        def sems(name, n):
            return [sem(f"{name}{i}") for i in range(n)]

        def sbuf(name, shape, dt=F32):
            return ctx.enter_context(nc.sbuf_tensor(name, shape, dt))

        z_d = dram("z_t", [Z_ALL, P, SEQ])
        rel_d = dram("rel_v", [HEADS, CHUNK, REL])
        sv_d = dram("sv_n", [CHUNK + SEQ, KVH * HD])
        lr_d = dram("lr_t", [RANK, SEQ])
        kv_d = dram("kv_n", [SEQ, 3 * SL])
        o_d = dram("o_n", [SEQ, D])
        b_d = dram("b_t", [PAIRS, P, SEQ])
        a_d = dram("a_n", [SEQ, D])
        x1_d = dram("x1_n", [SEQ, D])
        z2_d = dram("z2_n", [SEQ, D])
        slot_d = dram("slot_tok", [MAXB * P, 2], I32)
        y_d = dram("y_n", [2 * SEQ + P, D])

        act_h = sbuf("act_h", [P, KC, SEQ], F32R)
        act_l = sbuf("act_l", [P, KC, SEQ], F32R)
        wgt_h = sbuf("wgt_h", [P, KC, SL], F32R)
        wgt_l = sbuf("wgt_l", [P, KC, SL], F32R)
        blk_h = sbuf("blk_h", [P, KC + FC, P], F32R)
        blk_l = sbuf("blk_l", [P, KC + FC, P], F32R)
        cst = sbuf("cst", [P, K_ALL])
        toki = sbuf("toki", [P, 2, NT, 2], I32)
        arena = sbuf("arena", [P, ARENA])
        ident = cst[:, K_ID:K_ID + P]

        KEEP = ARENA - 96

        def region(at):
            end = ARENA if at == KEEP else KEEP
            mark = [at]

            def take(*shape, rows=P, dt=F32):
                n = int(np.prod(shape))
                assert mark[0] + n <= end, mark[0] + n
                v = arena[0:rows, mark[0]:mark[0] + n]
                mark[0] += n
                if dt != F32:
                    v = v.bitcast(dt)
                names = "abcd"[:len(shape)]
                if len(shape) > 1:
                    v = v.rearrange(f"p ({' '.join(names)}) -> p {' '.join(names)}",
                                    **{c: s for c, s in zip(names[:-1], shape)})
                return v
            return take

        SLOT = KC * SL
        raw = arena[:, 0:2 * SLOT].rearrange("p (s k n) -> p s k n", s=2, k=KC)
        take = region(2 * SLOT)
        ev = [take(SL) for _ in range(2)]
        AREA = 2 * SLOT + 2 * SL
        keep = region(KEEP)
        slot_i = keep(2, NT, dt=I32)
        slot_w = keep(2, NT)
        be_row = keep(MAXB, rows=1, dt=I32)
        nb_i = keep(1, dt=I32)
        idx, idy = keep(1, dt=I32), keep(1, dt=I32)

        take = region(AREA)
        kT = take(KVH, CHUNK + SEQ)
        bias = take(2, PAIRS * P)
        sc_s = take(PAIRS * P)
        pr_s = take(PAIRS * P)
        pT_s = take(PAIRS * P)
        qst = [take(PAIRS, P) for _ in range(2)]
        kst = take(KVH, P)
        vst = [take(KVH * HD) for _ in range(2)]
        oT_s = take(PAIRS, P)
        sink = take(PAIRS)
        gbias = take(2 * KC)
        s_mx, s_sd, s_es, s_den = (take(PAIRS) for _ in range(4))
        relt = oT_s[0:32, 0, 0:HEADS]
        buck = qst[0][0:32, 0:2, :].rearrange("p a b -> p (a b)")[:, 0:REL]
        relv = qst[1][0:HEADS, 0:2, :].rearrange("p a b -> p (a b)")[:, 0:REL]
        x_nat = [pr_s, pT_s]

        take = region(AREA)
        kvst = [take(3 * SL) for _ in range(2)]
        lrst = [take(P, rows=32) for _ in range(2)]
        gqst = [take(GH, P) for _ in range(2)]
        gup = take(GH * GK, rows=32)
        gla_l, gla_t, kdec = take(SL), take(SL), take(SL)
        st_a, st_b = take(GH, GV), take(GH, GV)
        o_s, o_q = take(GH * GV), take(GH * GV)
        gam = take(GH, 2)
        ssq = take(NT, GH)
        rsil = [take(SL) for _ in range(2)]
        opc = [take(SL) for _ in range(2)]
        apc = [take(SL) for _ in range(2)]
        rtmp = [take(SL) for _ in range(2)]
        ng_bc = kvst[0][:, 0:D]

        take = region(AREA)
        nat = [take(D) for _ in range(2)]
        gld = [take(SL) for _ in range(2)]
        gsg = [take(SL) for _ in range(2)]
        mtmp = [take(SL) for _ in range(2)]
        mT = take(KC, SEQ)
        take = region(AREA + 2 * D)
        xpc = [take(SL) for _ in range(2)]
        stats = take(NT, NS, 6)
        mv = take(NT, 2)
        rstd, nmr = take(NT), take(NT)
        ln_g, ln_b = take(D), take(D)
        xn = [take(D) for _ in range(2)]
        y_n = take(NT, D)

        take = region(AREA + 2 * D)
        lgT = take(SEQ)
        pnat = [take(PLE) for _ in range(2)]
        pT = take(PKC, SEQ)
        wple = take(PKC, D)
        pg_bc = take(D)
        gpre = [take(SL) for _ in range(2)]
        ptmp = [take(SL) for _ in range(2)]
        z2p = [take(SL) for _ in range(2)]
        x1p = [take(SL) for _ in range(2)]
        rb_bc = take(NLOG)
        lg = take(NT, NLOG)
        g_mx, g_ix, g_sum = take(NT), take(NT), take(NT)
        g_e, g_oh = take(NT, NG), take(NT, NG)
        e_all = take(NT, NE)
        e_sel, e_t, e_m = take(NT, EPG), take(NT, EPG), take(NT, EPG)
        e_oh = [take(NT, EPG) for _ in range(2)]
        e_mx = [take(NT) for _ in range(2)]
        oh = [take(NT, NE) for _ in range(2)]
        ohs = take(NT, NE)
        rank, pre, rt = take(NT, NE), take(NT, NE), take(NT, NE)
        cnt, nbk, bend, btmp = take(NE), take(NE), take(NE), take(NE)
        slot_f = take(NT)
        take = region(AREA)
        be_cmp = take(MAXB, NE, rows=1)
        be_f = take(MAXB, rows=1)

        u_h = act_h[:, 0:4, :].rearrange("p a b -> p (a b)").rearrange("p (k n) -> p k n", k=KC)
        u_l = act_l[:, 0:4, :].rearrange("p a b -> p (a b)").rearrange("p (k n) -> p k n", k=KC)
        d_h, d_l = act_h[:, 4:8, :], act_l[:, 4:8, :]
        ring = arena[:, 0:RING * SLOT]
        ring_up = ring.rearrange("p (r k n) -> p r k n", r=RING, k=KC)
        ring_down = ring.rearrange("p (r k n) -> p r k n", r=RING, k=FC)
        take = region(RING * SLOT)
        sig = take(SL)
        hid = take(SL)
        y_s = take(D)
        xb = take(D)
        slots = take(MAXB, 2, dt=I32)
        take = region(0)
        zt = [take(D) for _ in range(NT)]
        assert NT * D <= 2 * SLOT
        y0 = [take(D) for _ in range(NT // 2)]
        y1 = [take(D) for _ in range(NT // 2)]
        zn = [take(D) for _ in range(2)]
        zo = [take(D) for _ in range(2)]
        l2g, l2b = take(D), take(D)
        fst, fmv = take(2, 2, 6), take(2, 2)
        frs, fnm = take(2, 1), take(2, 1)

        ps = ctx.enter_context(nc.psum_tensor("ps", [P, 8, SL], F32))

        cst_ld, c_ld = sem("cst_loaded"), sem("constants_loaded")
        w_loaded, w_hi, w_lo, w_used = sem("w_loaded"), sem("w_hi"), sem("w_lo"), sem("w_used")
        n_loaded = sems("nat_loaded", 2)
        x1_ready = sems("x1_ready", 2)
        x1_stored = sems("x1_stored", 2)
        tp_done, tp_hi, tp_lo = sem("tp_done"), sem("tp_hi"), sem("tp_lo")
        pj_done, pj_free = sems("pj_done", 2), sems("pj_free", 2)
        ev_stored = sems("ev_stored", 2)
        rel_mm, rel_ev, rel_st, bias_ld = (
            sem(n) for n in ("rel_mm", "rel_ev", "rel_st", "bias_ld"))
        kt_pad = sem("kt_pad")
        q_ld, v_ld = sems("q_ld", 2), sems("v_ld", 2)
        k_st, sc_done, mx_ok, e_ok, p_ok, pt_done, pt_ev, pv_done, ot_ev, ot_st = (
            sem(n) for n in ("k_staged", "scores_done", "max_ok", "exp_ok", "probs_ok", "pt_done",
                             "pt_evacuated", "pv_done", "ot_evacuated", "ot_stored"))
        gu_ld, gu_one = sem("gate_up_norm_ld"), sem("gate_up_one")
        g_ld = sems("gla_ld", 2)
        gg_mm, gg_abs, gg_la, gg_suf, gg_dec, gg_kd, gu_mm, gs_up, go_mm, go_sq, go_ev, go_st = (
            sem(n) for n in ("glog_mm", "glog_ev", "glog_ok", "suffix_mm", "decay_ok", "kdec_ok",
                             "update_mm", "state_ok", "o_mm", "o_squared", "o_evacuated", "o_stored"))
        o_ld, a_ok, rs_v, rs_s = (
            sems("o_ld", 2), sems("a_ok", 2), sem("rs_var"), sem("rs_sqrt"))
        a_st = sems("a_stored", 2)
        gt_ld, gt_free = sems("gate_ld", 2), sems("gate_ready", 2)
        b_ld, m_ok = sems("b_ld", 2), sem("merged_ok")
        xp_ld = sems("x_piece_ld", 2)
        ln_ld, ln_v, ln_s, ln_r, xn_ok = (
            sem("ln1_ld"), sem("ln1_var"), sem("ln1_sqrt"), sem("ln1_rstd"), sem("xn_ok"))
        p_ld, p_tp, p_ev, pw_ld = sems("p_ld", 2), sem("p_tp"), sem("p_ev"), sem("ple_w_ld")
        lg_tp, r_mx, r_ex, r_dif, r_e2, r_oh, r_mm = (
            sem(n) for n in ("lg_tp", "r_max", "r_exp", "r_dif", "r_e2", "r_onehot", "r_mm"))
        zs_st, slots_ok, scat, nb_ok = (
            sem(n) for n in ("slots_empty", "slots_ok", "scattered", "blocks_ok"))
        pp_done, pp_free = sems("pp_done", 2), sems("pp_free", 2)
        gs_ok, z2_ok = sems("gsig_ok", 2), sems("z2_ok", 2)
        z2_st = sems("z2_st", 2)
        x1_ld = sems("x1_piece_ld", 2)
        m_ld, m_hi, m_lo, m_used = sems("moe_ld", 3), sems("moe_hi", 3), sems("moe_lo", 3), sems("moe_used", 3)
        idx_ok, xb_ld, xt_done, xt_hi, xt_lo = (
            sem(n) for n in ("idx_ok", "xb_ld", "xt_done", "xt_hi", "xt_lo"))
        gm_done, um_done, sl_ok, h_ok, ht_done, ht_hi, ht_lo, y_done, y_ev, y_st = (
            sem(n) for n in ("gate_done", "up_done", "silu_ok", "h_ok", "ht_done", "ht_hi", "ht_lo",
                             "y_done", "y_evacuated", "slots_y_stored"))
        l2_ld, z_ld, f_g, f_z = sem("ln2_ld"), sem("z2_ld"), sem("f_gained"), sems("y_ld", NT // 2)
        f_var, f_sq, f_rs, f_n, f_o = sem("f_var"), sem("f_sqrt"), sem("f_rstd"), sem("f_normed"), sems("f_out", 2)
        f_st = sems("f_stored", 2)
        t_sp, t_act, t_pe, t_dve, t_pool = (sem(f"tick_{n}") for n in ("sp", "act", "pe", "dve", "pool"))
        act_own, dve_own = sem("act_own"), sem("dve_own")

        w_in = a["w_in"][0]

        def cols(w, c, n=SL):
            return w[:, bass.ds(c, n)].rearrange("(k p) n -> p k n", p=P)

        def bcast(v, n):
            return bass.AP(tensor=v.tensor, offset=v.offset, ap=[[0, P], [1, n]])

        def bank(b, n=1):
            return ps[:, b:b + n, :].rearrange("p a n -> p (a n)")

        def arrived(view, m, b, chunks):
            return view[:, bass.ds((b * 3 + m) % RING, 1), chunks, :].rearrange("p a k n -> p (a k) n")

        def f(v):
            return v.bitcast(F32)

        block = ctx.enter_context(nc.Block())

        def loaded(s):
            return s * 16 + (16 if not isinstance(s, int) or s < S_RT else 16 * (1 + NG))

        @block.sync
        def _(sp):
            def slot_free(s):
                if not isinstance(s, int) or s > 0:
                    sp.wait_ge(w_loaded, loaded(s - 1))
                    sp.sem_inc(t_sp, 1)
                if not isinstance(s, int) or s > 1:
                    sp.wait_ge(w_lo, s * WC - WC)
                    sp.sem_inc(t_sp, 1)

            def load_slice(s, src, n=SL):
                slot_free(s)
                dst = raw[:, s % 2, :, 0:n] if isinstance(s, int) else (
                    raw[:, bass.ds(s % 2, 1), :, 0:n].rearrange("p a k n -> p (a k) n"))
                sp.dma_start(dst, src).then_inc(w_loaded, 16)

            def load_nat(u, j, src, dst):
                sp.wait_ge(tp_done, u * 2 + 2)
                sp.sem_inc(t_sp, 1)
                sp.dma_start(dst, src).then_inc(n_loaded[j], 16)

            def tile(x, t, n=D):
                return x[bass.ds(t * P, P), 0:n]

            x = a["x"][0]
            sp.dma_start(cst[:, :], a["cst"]).then_inc(cst_ld, 16)
            for u in range(2):
                load_nat(u, u, tile(x, u), x_nat[u])
            load_slice(0, cols(w_in, C_SQ))
            with sp.Fori(1, NT // 2) as v:
                for j in range(2):
                    load_nat(v * 2 + j, j, tile(x, v * 2 + j), x_nat[j])
            load_slice(1, cols(w_in, C_SQ + SL))
            sp.dma_start(toki[:, :], a["toki"]).then_inc(c_ld, 16)
            sp.dma_start(slot_d, a["empty"]).then_inc(zs_st, 16)
            sp.dma_start(relt, a["rel_table"]).then_inc(c_ld, 16)
            sp.dma_start(buck, a["bucket"]).then_inc(c_ld, 16)
            with nc.allow_non_contiguous_dma(reason="a value for each channel or head on its partition"):
                sp.dma_start(gbias, a["branch_gate_b"].rearrange("l t (c p) -> p (l t c)", p=P)).then_inc(c_ld, 16)
                for r in range(2):
                    s0 = a["swa_sinks"]
                    sp.dma_start(sink[CHUNK * r:CHUNK * (r + 1), :],
                                 bass.AP(tensor=s0.tensor, offset=s0.offset + r, ap=[[0, CHUNK], [2, PAIRS]])
                                 ).then_inc(c_ld, 16)
            sp.wait_ge(rel_st, 16)
            for r in range(2):
                sp.dma_start(bias[CHUNK * r:CHUNK * (r + 1), 1, :].rearrange("p (h k) -> p h k", h=PAIRS),
                             bass.AP(tensor=rel_d.tensor, offset=r * CHUNK * REL + CHUNK - 1,
                                     ap=[[REL - 1, CHUNK], [2 * CHUNK * REL, PAIRS], [1, P]])).then_inc(bias_ld, 16)
            load_slice(S_SKV, cols(w_in, C_SK))
            with sp.Fori(0, 4) as i:
                load_slice(i + S_GATE, cols(w_in, i * SL + C_GA))
            load_slice(S_GQ, cols(w_in, C_GQ))
            load_slice(S_LR, cols(w_in, C_LR, P), P)
            with sp.Fori(0, 3) as i:
                load_slice(i + S_KV, cols(w_in, i * SL + C_GK))
            for i in range(NS):
                load_slice(i + S_R, cols(w_in, i * SL + C_R))
            load_slice(S_WG, cols(a["w_branch_gla"][0], 0))

            sp.wait_ge(gu_one, 2)
            sp.dma_start(gup[0:RANK, :], a["gla_gate_up"][0]).then_inc(gu_ld, 16)
            sp.dma_start(gup[RANK:RANK + 1, :], a["gla_gate_b"]).then_inc(gu_ld, 16)
            for h in range(2):
                sp.wait_ge(ev_stored[h], 16 * (E_KV + 12))

            def gla_loads(t, j):
                sp.dma_start(kvst[j], kv_d[bass.ds(t * P, P), :]).then_inc(g_ld[j], 16)
                sp.dma_start(lrst[j][0:RANK, :], lr_d[:, bass.ds(t * P, P)]).then_inc(g_ld[j], 16)
                sp.dma_start(gqst[j], z_d[Z_GQ:Z_GQ + GH, :, bass.ds(t * P, P)].rearrange("h p n -> p h n")
                             ).then_inc(g_ld[j], 16)

            def gla_store(t):
                sp.wait_ge(go_ev, t + 1)
                sp.sem_inc(t_sp, 1)
                sp.dma_start(o_d[bass.ds(t * P, P), :], o_s).then_inc(go_st, 16)
            for j in range(2):
                gla_loads(j, j)
            with sp.Fori(1, NT // 2) as v:
                for j in range(2):
                    gla_store(v * 2 + (j - 2))
                    gla_loads(v * 2 + j, j)
            for t in range(NT - 2, NT):
                gla_store(t)
            sp.dma_start(ng_bc, bcast(a["gla_norm_g"], D)).then_inc(gu_ld, 16)
            sp.wait_ge(go_st, 16 * (NT + 1))
            for i in range(NS):
                for t in range(NT):
                    k = i * (NT // 2) + t // 2
                    if k:
                        sp.wait_ge(a_ok[t % 2], k)
                    sp.dma_start(opc[t % 2], o_d[t * P:(t + 1) * P, i * SL:(i + 1) * SL]).then_inc(o_ld[t % 2], 16)
            for j in range(2):
                sp.wait_ge(a_st[j], 16 * NT)
            with sp.Fori(NT // 2, NT) as v:
                for j in range(2):
                    load_nat(v * 2 + j, j, tile(a_d, v * 2 + (j - NT)), nat[j])

            def gates(base, src, s):
                for i in range(NS):
                    for c in range(CPS):
                        for h in range(2):
                            k = base + i * CPS + c
                            if k:
                                sp.wait_ge(gt_free[h], k)
                            sp.dma_start(gld[h], z_d[Z_GATE + k, :, h * SL:(h + 1) * SL]).then_inc(gt_ld[h], 16)
                    if i == 0:
                        load_slice(s, src)
            gates(0, cols(a["w_branch_gla"][0], SL), S_WG + 1)
            load_slice(S_WS, cols(a["w_branch_swa"][0], 0))
            for c in range(KC):
                sp.wait_ge(tp_lo, TL_A + max(c - 1, 0))
                sp.dma_start(nat[c % 2], b_d[c]).then_inc(b_ld[c % 2], 16)
            gates(KC, cols(a["w_branch_swa"][0], SL), S_WS + 1)
            load_slice(S_WO, cols(a["w_out"][0], 0))
            sp.wait_ge(tp_lo, TL_M)
            sp.dma_start(ln_g, bcast(a["ln1_g"], D)).then_inc(ln_ld, 16)
            sp.dma_start(ln_b, bcast(a["ln1_b"], D)).then_inc(ln_ld, 16)
            for i in range(NS):
                for t in range(NT):
                    k = i * (NT // 2) + t // 2
                    if k:
                        sp.wait_ge(pj_free[t % 2], B_WO + k + 1)
                    sp.dma_start(xpc[t % 2], x[t * P:(t + 1) * P, i * SL:(i + 1) * SL]).then_inc(xp_ld[t % 2], 16)
                if i == 0:
                    load_slice(S_WO + 1, cols(a["w_out"][0], SL))
            slot_free(S_RT)
            rt_w = raw[:, S_RT % 2]
            with nc.allow_non_contiguous_dma(reason="a router's few columns"):
                sp.dma_start(rt_w[:, :, 0:NG], a["router_group_w"][0].rearrange("(k p) n -> p k n", p=P)
                             ).then_inc(w_loaded, 16)
                for g in range(NG):
                    sp.dma_start(rt_w[:, :, NG + EPG * g:NG + EPG * (g + 1)],
                                 a["router_expert_w"][0, g].rearrange("(k p) n -> p k n", p=P)).then_inc(w_loaded, 16)
            load_slice(S_PG, cols(a["w_ple_gate"][0], 0))
            sp.wait_ge(tp_lo, TL_X1)
            for j in range(2):
                sp.wait_ge(x1_stored[j], 16 * (NT // 2))
            sp.dma_start(rb_bc[:, 0:NG], bcast(a["router_group_b"], NG)).then_inc(pw_ld, 16)
            sp.dma_start(rb_bc[:, NG:NLOG], bcast(a["router_expert_b"], NE)).then_inc(pw_ld, 16)
            sp.dma_start(wple, a["w_ple"][0].rearrange("(k p) n -> p k n", p=P)).then_inc(pw_ld, 16)
            sp.dma_start(pg_bc, bcast(a["ple_gate_b"], D)).then_inc(pw_ld, 16)
            for t in range(NT):
                if t > 1:
                    sp.wait_ge(p_ev, t - 1)
                sp.dma_start(pnat[t % 2], a["p"][0, 0, t * P:(t + 1) * P, :]).then_inc(p_ld[t % 2], 16)
            for i in range(NS):
                for t in range(NT):
                    k = i * (NT // 2) + t // 2
                    if k:
                        sp.wait_ge(z2_ok[t % 2], k)
                    sp.dma_start(x1p[t % 2], x1_d[t * P:(t + 1) * P, i * SL:(i + 1) * SL]).then_inc(x1_ld[t % 2], 16)
                if i == 0:
                    load_slice(S_PG + 1, cols(a["w_ple_gate"][0], SL))

            def block_loads(b, b_first=None):
                e = sp.value_load(be_row[0:1, bass.ds(b, 1)], min_val=0, max_val=NE - 1)
                for m, w in enumerate((a["expert_w_gate"], a["expert_w_up"], a["expert_w_down"])):
                    src = w[0, bass.ds(e, 1)].rearrange("e (p k) n -> p e (k n)", p=P)
                    if b_first is not None:
                        if m == 0:
                            sp.wait_ge(w_lo, WC * S_END)
                        elif b_first == 0 and m == 2:
                            for j in range(2):
                                sp.wait_ge(z2_st[j], 16 * NT)
                        if b_first == 1 and m == 2:
                            sp.wait_ge(m_lo[0], WC)
                    else:
                        sp.wait_ge(m_lo[(m + 1) % 3], (b + (m == 2) + -1) * WC)
                        sp.sem_inc(t_sp, 1)
                    if b_first != 0:
                        sp.wait_ge(m_ld[m], b * 16)
                        sp.sem_inc(t_sp, 1)
                    dst = ring.rearrange("p (r n) -> p r n", r=RING)[:, bass.ds((b * 3 + m) % RING, 1), :]
                    sp.dma_start(dst, src).then_inc(m_ld[m], 16)
            sp.wait_ge(nb_ok, 1)
            n_blocks = sp.snap(sp.value_load(nb_i[0:1, 0:1], min_val=0, max_val=MAXB - MINB) + MINB)
            block_loads(0, 0)
            block_loads(1, 1)
            with sp.Fori(2, n_blocks) as b:
                block_loads(b)
            for m in range(3):
                sp.wait_ge(m_lo[m], n_blocks * WC)
                sp.sem_inc(t_sp, 1)
            for t in range(NT):
                sp.dma_start(zt[t], z2_d[t * P:(t + 1) * P, :]).then_inc(z_ld, 16)
            sp.wait_ge(y_st, n_blocks * 16 + 16)
            sp.sem_inc(t_sp, 1)
            sp.dma_start(l2g, bcast(a["ln2_g"], D)).then_inc(l2_ld, 16)
            sp.dma_start(l2b, bcast(a["ln2_b"], D)).then_inc(l2_ld, 16)

            def load_y(t):
                for c, y in enumerate((y0, y1)):
                    sp.dma_start(y[t % (NT // 2)], y_d[c * SEQ + t * P:c * SEQ + (t + 1) * P, :]
                                 ).then_inc(f_z[t % (NT // 2)], 16)
            for t in range(NT // 2):
                load_y(t)
            for t in range(NT):
                if t + NT // 2 < NT:
                    sp.wait_ge(f_var, t + 1)
                    load_y(t + NT // 2)
                sp.wait_ge(f_o[t % 2], t // 2 + 1)
                sp.dma_start(a["out"][0, t * P:(t + 1) * P, :], zo[t % 2]).then_inc(f_st[t % 2], 16)
            for j in range(2):
                sp.wait_ge(f_st[j], 16 * (NT // 2))

        @block.gpsimd
        def _(pool):
            def store(h, n, dst, src):
                pool.wait_ge(pj_free[h], n + 2)
                pool.dma_start(dst, src).then_inc(ev_stored[h], 16)

            def halves(h):
                return slice(h * SL, (h + 1) * SL)

            pool.memset(kT[:, :, 0:CHUNK], 0.0).then_inc(kt_pad, 1)
            pool.wait_ge(kt_pad, 1)
            pool.dma_start(sv_d[0:CHUNK, :].rearrange("p (h d) -> p h d", h=KVH), kT[0:CHUNK, :, 0:CHUNK]
                           ).then_inc(ot_st, 16)
            pool.wait_ge(rel_ev, 1)
            pool.dma_start(rel_d, relv[:, None, :].to_broadcast([HEADS, CHUNK, REL])).then_inc(rel_st, 16)
            for i in range(NS):
                for c in range(CPS):
                    for h in range(2):
                        n = i * CPS + c
                        store(h, B_SQ + n, z_d[Z_SQ + n, :, halves(h)], ev[h])
            for t in range(NT):
                store(t % 2, B_SV + t // 2, sv_d[CHUNK + t * P:CHUNK + (t + 1) * P, :], ev[t % 2][:, 0:KVH * HD])

            def load_q(tile, j):
                pool.dma_start(qst[j], z_d[Z_SQ:Z_SQ + PAIRS, :, bass.ds(tile * P, P)].rearrange("h p n -> p h n")
                               ).then_inc(q_ld[j], 16)
            for h in range(2):
                pool.wait_ge(ev_stored[h], 16 * E_GATE)
            pool.wait_ge(ot_st, 16)
            pool.wait_ge(rel_st, 16)
            for h in range(2):
                pool.wait_ge(pj_free[h], B_SV + 1)
            load_q(0, 0)
            pool.tensor_copy(kst, kT[:, :, 0:P]).then_inc(k_st, 1)
            with pool.Fori(0, 4) as i:
                for j in range(4):
                    n = i * 4 + j
                    pool.wait_ge(sc_done, n + 2)
                    pool.sem_inc(t_pool, 1)
                    pool.tensor_copy(kst, kT[:, :, bass.ds((n + 1) % (2 * NT) * CHUNK, P)]).then_inc(k_st, 1)
                    if j % 2:
                        load_q((i * 2 + (j + 1) // 2) % NT, (j + 1) // 2 % 2)
                    pool.wait_ge(pv_done, n + 1)
                    pool.sem_inc(t_pool, 1)
                    pool.dma_start(vst[j % 2], sv_d[bass.ds(n * CHUNK, P), :]).then_inc(v_ld[j % 2], 16)
                    for h in range(2):
                        pool.wait_ge(pj_free[h], n + (B_GATE + 2))
                        pool.sem_inc(t_pool, 1)
                        pool.dma_start(z_d[bass.ds(n + Z_GATE, 1), :, halves(h)].rearrange("a p n -> p (a n)"),
                                       ev[h]).then_inc(ev_stored[h], 16)
                    if j % 2:
                        pool.wait_ge(ot_ev, n + 1)
                        pool.sem_inc(t_pool, 1)
                        pool.dma_start(b_d[:, :, bass.ds((i * 2 + j // 2) * P, P)].rearrange("h p n -> p h n"),
                                       oT_s).then_inc(ot_st, 16)
            pool.wait_ge(ot_st, 16 * (NT + 1))
            pool.wait_ge(q_ld[0], 16 * (NT // 2 + 1))
            pool.wait_ge(k_st, 2 * NT + 1)
            for j in range(2):
                pool.memset(lrst[j], 1.0).then_inc(gu_one, 1)
            for c in range(CPS):
                for h in range(2):
                    store(h, B_GQ + c, z_d[Z_GQ + c, :, halves(h)], ev[h])
            for h in range(2):
                store(h, B_LR, lr_d[:, halves(h)], ev[h][0:RANK, :])
            with pool.Fori(0, 3) as i:
                for t in range(NT):
                    pool.wait_ge(pj_free[t % 2], i * (NT // 2) + (B_KV + t // 2 + 2))
                    pool.sem_inc(t_pool, 1)
                    pool.dma_start(kv_d[t * P:(t + 1) * P, bass.ds(i * SL, SL)], ev[t % 2]
                                   ).then_inc(ev_stored[t % 2], 16)

            for i in range(NS):
                for t in range(NT):
                    pool.wait_ge(a_ok[t % 2], i * (NT // 2) + t // 2 + 1)
                    pool.dma_start(a_d[t * P:(t + 1) * P, i * SL:(i + 1) * SL], apc[t % 2]).then_inc(a_st[t % 2], 16)
            for t in range(NT):
                pool.wait_ge(x1_ready[t % 2], t // 2 + 1)
                pool.dma_start(x1_d[t * P:(t + 1) * P, :], nat[t % 2]).then_inc(x1_stored[t % 2], 16)

            pool.wait_ge(zs_st, 16)
            pool.wait_ge(c_ld, CONSTS)
            for i in range(NS):
                if i == 1:
                    pool.wait_ge(slots_ok, 2)
                    for c in range(2):
                        for t in range(NT):
                            pool.indirect_dma_start(
                                out=slot_d, out_offset=bass.IndirectOffsetOnAxis(ap=slot_i[:, c, t:t + 1], axis=0),
                                in_=toki[:, c, t, :], in_offset=None).then_inc(scat, 16)
                for t in range(NT):
                    pool.wait_ge(z2_ok[t % 2], i * (NT // 2) + t // 2 + 1)
                    pool.dma_start(z2_d[t * P:(t + 1) * P, i * SL:(i + 1) * SL], z2p[t % 2]).then_inc(z2_st[t % 2], 16)
            pool.wait_ge(scat, 16 * 2 * NT)
            for j in range(2):
                pool.wait_ge(z2_st[j], 16 * NT)
                pool.wait_ge(x1_stored[j], 16 * (NT // 2))

            n_blocks = pool.snap(pool.value_load(nb_i[0:1, 0:1], min_val=0, max_val=MAXB - MINB) + MINB)

            with nc.allow_non_contiguous_dma(reason="two numbers of each slot"):
                pool.dma_start(slots, slot_d.rearrange("(b p) c -> p b c", p=P)).then_inc(y_st, 16)
            pool.wait_ge(y_st, 16)

            def gather(b, k):
                pool.tensor_copy(idx, slots[:, bass.ds(b, 1), 0]).then_inc(idx_ok, 1)
                pool.wait_ge(idx_ok, k + 1)
                pool.sem_inc(t_pool, 1)
                pool.indirect_dma_start(out=xb, out_offset=None, in_=x1_d,
                                        in_offset=bass.IndirectOffsetOnAxis(ap=idx, axis=0)).then_inc(xb_ld, 16)

            def scatter(b, k):
                pool.wait_ge(y_st, b * 16 + 16)
                pool.sem_inc(t_pool, 1)
                pool.tensor_copy(idy, slots[:, bass.ds(b, 1), 1]).then_inc(idx_ok, 1)
                pool.wait_ge(idx_ok, k + 1)
                pool.sem_inc(t_pool, 1)
                pool.wait_ge(y_ev, b * 2 + 4)
                pool.sem_inc(t_pool, 1)
                pool.indirect_dma_start(out=y_d, out_offset=bass.IndirectOffsetOnAxis(ap=idy, axis=0),
                                        in_=y_s, in_offset=None).then_inc(y_st, 16)
            gather(0, 0)
            for b in range(1, 3):
                pool.wait_ge(xt_done, 2 * b)
                gather(b, b)
            with pool.Fori(3, n_blocks) as b:
                pool.wait_ge(xt_done, b * 2)
                pool.sem_inc(t_pool, 1)
                gather(b, b * 2 + -3)
                scatter(b + -3, b * 2 + -2)
            for k in range(3):
                scatter(pool.snap(n_blocks + (k - 3)), n_blocks * 2 + (k - 3))

            pool.wait_ge(l2_ld, 32)
            for t in range(NT):
                j = t % 2
                pool.wait_ge(f_n, t + 1)
                pool.tensor_tensor(zn[j], zn[j], l2g, ALU.mult).then_inc(f_g, 1)
                pool.wait_ge(f_g, t + 1)
                if t > 1:
                    pool.wait_ge(f_st[j], 16 * (t // 2))
                pool.tensor_tensor(zo[j], zn[j], l2b, ALU.add).then_inc(f_o[j], 1)

        acts = (act_h, act_l)
        wgts = (wgt_h, wgt_l)
        THREE = ((0, 0), (0, 1), (1, 0))

        @block.tensor
        def _(pe):
            def one_pass(s, out, b, n, left, right, first, last):
                pe.wait_ge(pj_free[b], n + 1)
                pe.sem_inc(t_pe, 1)
                for k in range(KC):
                    if first and k % 2 == 0:
                        pe.wait_ge(w_lo, s * WC + (k // 2 + 1))
                        pe.sem_inc(t_pe, 1)
                    for x, y in THREE:
                        ins = pe.matmul(out, left(x, k), right(y, k), start=k == 0 and (x, y) == (0, 0),
                                        stop=k == KC - 1 and x == 1)
                    if last and k % 2 and k < KC - 1:
                        ins.then_inc(w_used, 1)
                ins.then_inc(pj_done[b], 1)

            def to_channels(s, c, h, n, first=False, last=False):
                one_pass(s, bank(h), h, n,
                         lambda x, k: wgts[x][:, k, c * P:(c + 1) * P],
                         lambda x, k: acts[x][:, k, h * SL:(h + 1) * SL], first, last)

            def to_tokens(s, t, n, first=False, last=False, c0=0, w=SL):
                one_pass(s, bank(t % 2)[:, 0:w], t % 2, n,
                         lambda x, k: acts[x][:, k, t * P:(t + 1) * P],
                         lambda x, k: wgts[x][:, k, c0:c0 + w], first, last)

            def slice_channels(s, n):
                for c in range(CPS):
                    for h in range(2):
                        to_channels(s, c, h, n + c, (c, h) == (0, 0), (c, h) == (CPS - 1, 1))

            def slice_tokens(s, n):
                for t in range(NT):
                    to_tokens(s, t, n + t // 2, t == 0, t == NT - 1)

            def transposes(src, q, low):
                pe.wait_ge(tp_lo, low)
                h = q % 2
                for k in range(KC // 2):
                    ins = pe.transpose(bank(2 + h)[:, k * P:(k + 1) * P],
                                       src[:, (h * 4 + k) * P:(h * 4 + k + 1) * P], ident)
                ins.then_inc(tp_done, 1)

            pe.sem_inc(tp_done, 4)
            pe.sem_inc(tp_lo, 2)
            for b in range(2):
                pe.sem_inc(pj_free[b], 1)
            pe.sem_inc(sc_done, 1)
            pe.sem_inc(pv_done, 2)

            pe.wait_ge(cst_ld, 16)
            with pe.Fori(0, NT // 2) as v:
                for j in range(2):
                    pe.wait_ge(n_loaded[j], v * 16 + 16)
                    pe.sem_inc(t_pe, 1)
                    for h in range(2):
                        pe.wait_ge(tp_lo, v * 4 + (2 * j + h + 1))
                        pe.sem_inc(t_pe, 1)
                        for k in range(KC // 2):
                            ins = pe.transpose(bank(2 + h)[:, k * P:(k + 1) * P],
                                               x_nat[j][:, (h * 4 + k) * P:(h * 4 + k + 1) * P], ident)
                        ins.then_inc(tp_done, 1)
            pe.wait_ge(c_ld, CONSTS)
            pe.matmul(ps[0:HEADS, 7, 0:REL], relt, buck, start=True, stop=True).then_inc(rel_mm, 1)

            pe.wait_ge(tp_lo, TL_X)
            with pe.Fori(0, NS) as i:
                slice_channels(i + S_SQ, i * CPS + B_SQ)
            for c in range(KVH // 2):
                for h in range(2):
                    to_channels(S_SKV, c, h, B_SK + c, (c, h) == (0, 0))
            for t in range(NT):
                to_tokens(S_SKV, t, B_SV + t // 2, False, t == NT - 1, c0=KVH * HD, w=KVH * HD)

            with pe.Fori(0, 4) as i:
                for j in range(4):
                    n = i * 4 + j
                    pe.wait_ge(q_ld[j // 2], i * 16 + 16)
                    pe.sem_inc(t_pe, 1)
                    pe.wait_ge(k_st, n + 1)
                    pe.sem_inc(t_pe, 1)
                    q = qst[j // 2]
                    for h4 in range(2):
                        for p4 in range(4):
                            for r in range(2):
                                p = ((h4 + r) % 2) * 4 + p4
                                lo = CHUNK * r
                                ins = pe.matmul(bank(4 + p // 4)[lo:lo + CHUNK, (p % 4) * P:(p % 4 + 1) * P],
                                                q[lo:lo + CHUNK, p, (j % 2) * CHUNK:(j % 2 + 1) * CHUNK],
                                                kst[lo:lo + CHUNK, p // 2, :], start=True, stop=True)
                    ins.then_inc(sc_done, 1)
                    for h in range(2):
                        to_channels(i + S_GATE, j, h, n + B_GATE, (j, h) == (0, 0), (j, h) == (3, 1))
                    pe.wait_ge(p_ok, n + 1)
                    pe.sem_inc(t_pe, 1)
                    for p in range(PAIRS):
                        ins = pe.transpose(bank(2 + p // 4)[:, (p % 4) * P:(p % 4 + 1) * P],
                                           pr_s[:, p * P:(p + 1) * P], ident)
                    ins.then_inc(pt_done, 1)
                    pe.wait_ge(v_ld[j % 2], i * 32 + 16 * (j // 2 + 1))
                    pe.sem_inc(t_pe, 1)
                    pe.wait_ge(pt_ev, n + 1)
                    pe.sem_inc(t_pe, 1)
                    pT3 = pT_s.rearrange("p (h n) -> p h n", h=PAIRS)
                    for r in range(2):
                        for g in range(KVH):
                            ins = pe.matmul(bank(6)[CHUNK * r:CHUNK * (r + 1), g * P:(g + 1) * P],
                                            vst[j % 2][:, g * HD:(g + 1) * HD],
                                            pT3[:, 2 * g:2 * g + 2, CHUNK * r:CHUNK * (r + 1)],
                                            start=True, stop=True)
                    ins.then_inc(pv_done, 1)

            slice_channels(S_GQ, B_GQ)
            for h in range(2):
                to_channels(S_LR, 0, h, B_LR, h == 0, h == 1)
            with pe.Fori(0, 3) as i:
                slice_tokens(i + S_KV, i * (NT // 2) + B_KV)

            for b in range(2):
                pe.wait_ge(pj_free[b], B_R + 1)
            pe.wait_ge(gu_ld, 32)
            with pe.Fori(0, NT // 2) as v:
                for j in range(2):
                    t = v * 2 + j
                    pe.wait_ge(g_ld[j], v * 48 + 48)
                    pe.sem_inc(t_pe, 1)
                    pe.matmul(bank(0), lrst[j][0:RANK + 1, :], gup[0:RANK + 1, :], start=True, stop=True
                              ).then_inc(gg_mm, 1)
                    pe.wait_ge(gg_la, t + 1)
                    pe.sem_inc(t_pe, 1)
                    for h in range(GH):
                        pe.matmul(bank(0)[:, 2 * h:2 * h + 2], gla_l[:, h * GK:(h + 1) * GK],
                                  cst[:, K_CH:K_CH + 2], start=True, stop=True)
                    pe.matmul(bank(1), cst[:, K_SUF:K_SUF + P], gla_l, start=True, stop=True).then_inc(gg_suf, 1)
                    pe.wait_ge(gg_kd, t + 1)
                    pe.sem_inc(t_pe, 1)
                    for c in range(2):
                        lo = CHUNK * c
                        for h in range(GH):
                            ins = pe.matmul(bank(2 + 2 * c, 2)[:, h * GV:(h + 1) * GV],
                                            kdec[lo:lo + CHUNK, h * GK:(h + 1) * GK],
                                            kvst[j][lo:lo + CHUNK, SL + h * GV:SL + (h + 1) * GV],
                                            start=True, stop=True)
                        ins.then_inc(gu_mm, 1)
                    for c, st in enumerate((st_a, st_b)):
                        pe.wait_ge(gs_up, t * 8 + 4 * (c + 1))
                        pe.sem_inc(t_pe, 1)
                        for h in range(GH):
                            ins = pe.matmul(bank(6, 2)[CHUNK * c:CHUNK * (c + 1), h * GV:(h + 1) * GV],
                                            gqst[j][:, h, CHUNK * c:CHUNK * (c + 1)], st[:, h, :],
                                            start=True, stop=True)
                    ins.then_inc(go_mm, 1)

            with pe.Fori(0, NS) as i:
                slice_tokens(i + S_R, i * (NT // 2) + B_R)
            with pe.Fori(0, NT // 2) as v:
                for j in range(2):
                    pe.wait_ge(n_loaded[j], v * 16 + 16 * (NT // 2 + 1))
                    pe.sem_inc(t_pe, 1)
                    for h in range(2):
                        pe.wait_ge(tp_lo, v * 4 + (TL_X + 2 * j + h - 1))
                        pe.sem_inc(t_pe, 1)
                        for k in range(KC // 2):
                            ins = pe.transpose(bank(2 + h)[:, k * P:(k + 1) * P],
                                               nat[j][:, (h * 4 + k) * P:(h * 4 + k + 1) * P], ident)
                        ins.then_inc(tp_done, 1)
            pe.wait_ge(tp_lo, TL_A)
            with pe.Fori(0, NS) as i:
                slice_channels(i + S_WG, i * CPS + B_WG)
            pe.wait_ge(tp_lo, TL_B)
            with pe.Fori(0, NS) as i:
                slice_channels(i + S_WS, i * CPS + B_WS)
            pe.wait_ge(tp_lo, TL_M)
            with pe.Fori(0, NS) as i:
                slice_tokens(i + S_WO, i * (NT // 2) + B_WO)
            with pe.Fori(0, NT // 2) as v:
                for j in range(2):
                    pe.wait_ge(x1_ready[j], v + 1)
                    pe.sem_inc(t_pe, 1)
                    for h in range(2):
                        pe.wait_ge(tp_lo, v * 4 + (TL_M + 2 * j + h - 1))
                        pe.sem_inc(t_pe, 1)
                        for k in range(KC // 2):
                            ins = pe.transpose(bank(2 + h)[:, k * P:(k + 1) * P],
                                               nat[j][:, (h * 4 + k) * P:(h * 4 + k + 1) * P], ident)
                        ins.then_inc(tp_done, 1)

            pe.wait_ge(tp_lo, TL_X1)
            for h in range(2):
                to_channels(S_RT, 0, h, B_RT, h == 0, h == 1)
            for t in range(NT):
                pe.wait_ge(p_ld[t % 2], 16 * (t // 2 + 1))
                if t > 1:
                    pe.wait_ge(p_ev, t - 1)
                for k in range(PKC):
                    ins = pe.transpose(bank(4 + t % 2)[:, k * P:(k + 1) * P], pnat[t % 2][:, k * P:(k + 1) * P], ident)
                ins.then_inc(p_tp, 1)
            for b in range(2):
                pe.wait_ge(pj_free[b], B_PG + 1)
            for t in range(NT):
                ins = pe.transpose(bank(2 + t // 4)[:, (t % 4) * P:(t % 4 + 1) * P], lgT[:, t * P:(t + 1) * P], ident)
            ins.then_inc(lg_tp, 1)
            pe.wait_ge(p_ev, NT)
            pe.wait_ge(pw_ld, 64)
            for b in range(2):
                pe.sem_inc(pp_free[b], 1)
            for i in range(NS):
                for t in range(NT):
                    n = i * (NT // 2) + t // 2
                    to_tokens(S_PG + i, t, B_PG + n, t == 0, t == NT - 1)
                    pe.wait_ge(pp_free[t % 2], n + 1)
                    for k in range(PKC):
                        ins = pe.matmul(bank(4 + t % 2), pT[:, k, t * P:(t + 1) * P],
                                        wple[:, k, i * SL:(i + 1) * SL], start=k == 0, stop=k == PKC - 1)
                    ins.then_inc(pp_done[t % 2], 1)
                if i == 0:
                    pe.wait_ge(r_oh, 1)
                    o2 = ohs.rearrange("p t e -> p (t e)")
                    pe.matmul(bank(6)[:, 0:NT * NE], cst[:, K_ERL:K_ERL + P], o2, start=True, stop=True)
                    pe.matmul(bank(7)[:, 0:NT * NE], cst[:, K_ONE:K_ONE + P], o2, start=True, stop=True
                              ).then_inc(r_mm, 1)

            blk = (blk_h, blk_l)
            xb3 = xb.rearrange("p (n k) -> p k n", k=KC)
            hid3 = hid.rearrange("p (n k) -> p k n", k=FC)
            uw, dw = (u_h, u_l), (d_h, d_l)

            def x_transposes(b):
                pe.wait_ge(xb_ld, b * 16 + 16)
                pe.sem_inc(t_pe, 1)
                for h in range(2):
                    for k in range(KC // 2):
                        ins = pe.transpose(bank(2 + h)[:, k * P:(k + 1) * P], xb3[:, h * 4 + k, :], ident)
                    ins.then_inc(xt_done, 1)

            def up_proj(b, m, w, done):
                for k in range(KC):
                    if k % 2 == 0:
                        pe.wait_ge(m_lo[m], b * WC + (k // 2 + 1))
                        pe.sem_inc(t_pe, 1)
                    for x, y in THREE:
                        ins = pe.matmul(bank(m), blk[x][:, k, :], w[y][:, k, :],
                                        start=k == 0 and (x, y) == (0, 0), stop=k == KC - 1 and x == 1)
                    if k % 2 and k < KC - 1:
                        ins.then_inc(m_used[m], 1)
                ins.then_inc(done, 1)

            def down_proj(b):
                pe.wait_ge(ht_lo, b + 1)
                pe.sem_inc(t_pe, 1)
                pe.wait_ge(y_ev, b * 2 + 2)
                pe.sem_inc(t_pe, 1)
                for k in range(FC):
                    pe.wait_ge(m_lo[2], b * WC + (k + 1))
                    pe.sem_inc(t_pe, 1)
                    for h in range(2):
                        for x, y in THREE:
                            ins = pe.matmul(bank(5 + h), blk[x][:, KC + k, :], dw[y][:, k, h * SL:(h + 1) * SL],
                                            start=k == 0 and (x, y) == (0, 0), stop=k == FC - 1 and x == 1)
                    if k < FC - 1:
                        ins.then_inc(m_used[2], 1)
                ins.then_inc(y_done, 1)

            def step(b, first, last):
                pe.wait_ge(xt_lo, b * 2 + 2)
                pe.sem_inc(t_pe, 1)
                if not first:
                    pe.wait_ge(sl_ok, b)
                    pe.sem_inc(t_pe, 1)
                up_proj(b, 0, wgts, gm_done)
                if not first:
                    pe.wait_ge(h_ok, b)
                    pe.sem_inc(t_pe, 1)
                up_proj(b, 1, uw, um_done)
                if not last:
                    x_transposes(b + 1)
                if not first:
                    down_proj(b - 1)
                pe.wait_ge(h_ok, b + 1)
                pe.sem_inc(t_pe, 1)
                for k in range(FC):
                    ins = pe.transpose(bank(4)[:, k * P:(k + 1) * P], hid3[:, k, :], ident)
                ins.then_inc(ht_done, 1)

            pe.sem_inc(y_ev, 2)
            pe.wait_ge(nb_ok, 1)
            last_b = pe.snap(pe.value_load(nb_i[0:1, 0:1], min_val=0, max_val=MAXB - MINB) + (MINB - 1))
            x_transposes(0)
            step(0, True, False)
            with pe.Fori(1, last_b) as b:
                step(b, False, False)
            step(last_b, False, True)
            down_proj(last_b)

        @block.scalar
        def _(act):
            own = Steps()

            def func(out, in_, f=ACT.Copy, **kw):
                return act.activation(out, in_, f, **kw)

            def split(s, n_last, w=SL):
                act.wait_ge(w_loaded, loaded(s))
                act.sem_inc(t_act, 1)
                for c in range(WC):
                    if c == WC - 1:
                        if n_last is not None:
                            act.wait_ge(pj_done[1], n_last + 1)
                            act.sem_inc(t_act, 1)
                    elif n_last is not None:
                        act.wait_ge(w_used, s * (WC - 1) + (c - 1) - (WC - 3))
                        act.sem_inc(t_act, 1)
                    src = raw[:, s % 2, 2 * c:2 * c + 2, 0:w] if isinstance(s, int) else (
                        raw[:, bass.ds(s % 2, 1), 2 * c:2 * c + 2, 0:w].rearrange("p a k n -> p (a k) n"))
                    func(wgt_h[:, 2 * c:2 * c + 2, 0:w], src).then_inc(w_hi, 1)

            def tile_high(t, h, q):
                act.wait_ge(tp_done, q)
                act.sem_inc(t_act, 1)
                func(act_h[:, 4 * h:4 * h + 4, bass.ds(t * P, P)],
                     bank(2 + h).rearrange("p (k n) -> p k n", k=4)).then_inc(tp_hi, 1)

            def evac(h, n, m, f=ACT.Copy, w=SL, **kw):
                act.wait_ge(pj_done[h], n + 1)
                act.sem_inc(t_act, 1)
                if not (isinstance(m, int) and m == 0):
                    act.wait_ge(ev_stored[h], m * 16)
                    act.sem_inc(t_act, 1)
                func(ev[h][:, 0:w], bank(h)[:, 0:w], f, **kw).then_inc(pj_free[h], 1)

            with act.Fori(0, NT // 2) as v:
                for j in range(2):
                    for h in range(2):
                        tile_high(v * 2 + j, h, v * 4 + (2 * j + h + 5))
            split(0, None)
            act.wait_ge(rel_mm, 1)
            func(relv, ps[0:HEADS, 7, 0:REL]).then_inc(rel_ev, 1)
            for i in range(NS):
                for c in range(CPS):
                    for h in range(2):
                        if (c, h) == (CPS - 1, 1):
                            split(i + 1, B_SQ + i * CPS + c)
                        n = i * CPS + c
                        evac(h, B_SQ + n, E_SQ + n, scale=HD ** -0.5)
            act.wait_ge(kt_pad, 1)
            for c in range(KVH // 2):
                for h in range(2):
                    act.wait_ge(pj_done[h], B_SK + c + 1)
                    for g in range(2):
                        for r in range(2):
                            ins = func(kT[r * HD:(r + 1) * HD, 2 * c + g, CHUNK + h * SL:CHUNK + (h + 1) * SL],
                                       bank(h)[g * HD:(g + 1) * HD, :])
                    ins.then_inc(pj_free[h], 1)
            for t in range(NT):
                if t == NT - 1:
                    split(S_GATE, B_SV + t // 2)
                evac(t % 2, B_SV + t // 2, E_SV + t // 2, w=KVH * HD)

            act.wait_ge(c_ld, CONSTS)
            with act.Fori(0, 4) as i:
                for j in range(4):
                    n = i * 4 + j
                    act.wait_ge(mx_ok, n + 1)
                    act.sem_inc(t_act, 1)
                    func(pr_s, sc_s, ACT.Exp)
                    func(s_es, s_sd, ACT.Exp).then_inc(e_ok, 1)
                    for h in range(2):
                        if (j, h) == (3, 1):
                            split(i + (S_GATE + 1), n + B_GATE)
                        evac(h, n + B_GATE, n + E_GATE, ACT.Identity,
                             bias=gbias[:, bass.ds(n, 1)])
                    act.wait_ge(pt_done, n + 1)
                    act.sem_inc(t_act, 1)
                    func(pT_s, bank(2, 2)).then_inc(pt_ev, 1)
            for c in range(CPS):
                for h in range(2):
                    if (c, h) == (CPS - 1, 1):
                        split(S_LR, B_GQ + c, P)
                    evac(h, B_GQ + c, E_GQ + c, scale=GK ** -0.5)
            evac(0, B_LR, E_LR)
            split(S_KV, B_LR)
            evac(1, B_LR, E_LR)
            with act.Fori(0, 3) as i:
                for t in range(NT):
                    n = i * (NT // 2) + t // 2
                    if t == NT - 1:
                        split(i + (S_KV + 1), n + B_KV)
                    evac(t % 2, n + B_KV, n + E_KV)

            with own.loop(act, NT, 2) as t:
                act.wait_ge(gg_mm, t + 1)
                act.sem_inc(t_act, 1)
                func(gla_t, bank(0), ACT.Abs).then_inc(act_own, 1)
                act.wait_ge(act_own, own.done())
                act.sem_inc(t_act, 1)
                func(gla_t, gla_t, ACT.Exp, scale=-1.0).then_inc(act_own, 1)
                act.wait_ge(act_own, own.done())
                act.sem_inc(t_act, 1)
                func(gla_t, gla_t, ACT.Ln, bias=1.0).then_inc(gg_abs, 1)
                act.wait_ge(gg_suf, t + 1)
                act.sem_inc(t_act, 1)
                func(gla_t, bank(1), ACT.Exp, scale=1.0 / TAU)
                func(gam.rearrange("p h c -> p (h c)"), bank(0)[:, 0:2 * GH], ACT.Exp, scale=1.0 / TAU
                     ).then_inc(gg_dec, 1)
                act.wait_ge(go_mm, t + 1)
                act.sem_inc(t_act, 1)
                func(o_q, bank(6, 2), ACT.Square).then_inc(go_sq, 1)
            act.wait_ge(rs_v, 1)
            func(ssq, ssq, ACT.Sqrt).then_inc(rs_s, 1)
            for i in range(NS):
                for t in range(NT):
                    n = i * (NT // 2) + t // 2
                    if t == NT - 1:
                        split(S_R + 1 + i, B_R + n)
                    act.wait_ge(pj_done[t % 2], B_R + n + 1)
                    if n:
                        act.wait_ge(a_ok[t % 2], n)
                    func(rsil[t % 2], bank(t % 2), ACT.Silu).then_inc(pj_free[t % 2], 1)
            with act.Fori(0, NT // 2) as v:
                for j in range(2):
                    for h in range(2):
                        tile_high(v * 2 + j, h, v * 4 + (2 * NT + 2 * j + h + 5))

            def sigmoids(base, nb, s):
                for i in range(NS):
                    for c in range(CPS):
                        for h in range(2):
                            k = base + i * CPS + c
                            act.wait_ge(gt_ld[h], 16 * (k + 1))
                            act.wait_ge(pj_free[h], nb + i * CPS + c + 1)
                            func(gsg[h], gld[h], ACT.Sigmoid).then_inc(gt_free[h], 1)
                            if (c, h) == (CPS - 1, 0):
                                split(s + 1 + i, nb + i * CPS + c)
            sigmoids(0, B_WG, S_WG)
            for c in range(KC):
                act.wait_ge(b_ld[c % 2], 16 * (c // 2 + 1))
                func(act_h[:, c, :], nat[c % 2]).then_inc(tp_hi, 1)
            sigmoids(KC, B_WS, S_WS)
            for c in range(KC):
                act.wait_ge(m_ok, 2 * KC)
                func(act_h[:, c, :], mT[:, c, :]).then_inc(tp_hi, 1)
            split(S_WO + 1, B_WO + 3)
            split(S_RT, B_WO + 7, NLOG)
            act.wait_ge(ln_v, 1)
            func(rstd, rstd, ACT.Sqrt).then_inc(ln_s, 1)
            act.wait_ge(ln_r, 1)
            for t in range(NT + 1):
                if t < NT:
                    if t > 1:
                        act.wait_ge(x1_ready[t % 2], t // 2)
                    func(xn[t % 2], y_n[:, t, :], ACT.Identity, bias=nmr[:, t:t + 1], scale=rstd[:, t:t + 1]
                         ).then_inc(xn_ok, 1)
                if t > 0:
                    for h in range(2):
                        tile_high(t - 1, h, 4 * NT + 2 * (t - 1) + h + 5)
            for h in range(2):
                act.wait_ge(pj_done[h], B_RT + 1)
                func(lgT[:, h * SL:(h + 1) * SL], bank(h)).then_inc(pj_free[h], 1)
            split(S_PG, B_RT)
            for t in range(NT):
                act.wait_ge(p_tp, t + 1)
                func(pT[:, :, t * P:(t + 1) * P], bank(4 + t % 2)[:, 0:PLE].rearrange("p (k n) -> p k n", k=PKC)
                     ).then_inc(p_ev, 1)
            act.wait_ge(r_mx, 1)
            func(g_e, g_e, ACT.Exp).then_inc(r_ex, 1)
            act.wait_ge(r_dif, 1)
            func(e_mx[1], e_mx[1], ACT.Exp).then_inc(r_e2, 1)
            for i in range(NS):
                for t in range(NT):
                    n = i * (NT // 2) + t // 2
                    act.wait_ge(pj_free[t % 2], B_PG + n + 2)
                    func(gpre[t % 2], gpre[t % 2], ACT.Sigmoid).then_inc(gs_ok[t % 2], 1)
                    if i == 0 and t == NT - 2:
                        split(S_PG + 1, B_PG + NT // 2 - 1)

            act.wait_ge(nb_ok, 1)
            last_b = act.snap(act.value_load(nb_i[0:1, 0:1], min_val=0, max_val=MAXB - MINB) + (MINB - 1))

            def split_expert(m, b, dst, src, done, free):
                act.wait_ge(m_ld[m], b * 16 + 16)
                act.sem_inc(t_act, 1)
                w = dst.shape[1] // WC
                for c in range(WC):
                    if free:
                        if c < WC - 1:
                            act.wait_ge(m_used[m], b * (WC - 1) + (c + 2 - WC))
                            act.sem_inc(t_act, 1)
                        else:
                            act.wait_ge(done, b)
                            act.sem_inc(t_act, 1)
                    func(dst[:, w * c:w * (c + 1), :], arrived(src, m, b, slice(w * c, w * (c + 1)))).then_inc(m_hi[m], 1)

            def x_high(b, free):
                if free:
                    act.wait_ge(um_done, b)
                    act.sem_inc(t_act, 1)
                for h in range(2):
                    act.wait_ge(xt_done, b * 2 + (h + 1))
                    act.sem_inc(t_act, 1)
                    func(blk_h[:, 4 * h:4 * h + 4, :], bank(2 + h).rearrange("p (k n) -> p k n", k=4)
                         ).then_inc(xt_hi, 1)

            def y_out(b):
                act.wait_ge(y_done, b + 1)
                act.sem_inc(t_act, 1)
                act.wait_ge(y_st, b * 16 + 16)
                act.sem_inc(t_act, 1)
                for h in range(2):
                    func(y_s[:, h * SL:(h + 1) * SL], bank(5 + h)).then_inc(y_ev, 1)

            def step(b, first, last):
                if not last:
                    split_expert(0, b + 1, wgt_h, ring_up, gm_done, True)
                act.wait_ge(gm_done, b + 1)
                act.sem_inc(t_act, 1)
                if not first:
                    act.wait_ge(h_ok, b)
                    act.sem_inc(t_act, 1)
                func(sig, bank(0), ACT.Silu).then_inc(sl_ok, 1)
                if not last:
                    split_expert(1, b + 1, u_h, ring_up, um_done, True)
                    x_high(b + 1, True)
                split_expert(2, b, d_h, ring_down, y_done, not first)
                if not first:
                    y_out(b - 1)
                act.wait_ge(ht_done, b + 1)
                act.sem_inc(t_act, 1)
                func(blk_h[:, KC:KC + FC, :], bank(4).rearrange("p (k n) -> p k n", k=FC)).then_inc(ht_hi, 1)

            act.wait_ge(pj_done[1], B_PG + NT)
            x_high(0, False)
            split_expert(0, 0, wgt_h, ring_up, gm_done, False)
            split_expert(1, 0, u_h, ring_up, um_done, False)
            step(0, True, False)
            with act.Fori(1, last_b) as b:
                step(b, False, False)
            step(last_b, False, True)
            y_out(last_b)

            for t in range(NT):
                j = t % 2
                act.wait_ge(f_var, t + 1)
                func(frs[:, j, :], frs[:, j, :], ACT.Sqrt).then_inc(f_sq, 1)
                if t > 1:
                    act.wait_ge(f_g, t - 1)
                    act.wait_ge(f_o[j], t // 2)
                act.wait_ge(f_rs, t + 1)
                func(zn[j], zt[t], ACT.Identity, bias=fnm[:, j, :], scale=frs[:, j, :]).then_inc(f_n, 1)

        @block.vector
        def _(dve):
            own = Steps()

            def over(v, n):
                return v[:, :, None].to_broadcast([v.shape[0], v.shape[1], n])

            def along(v, n):
                return v[:, None, :].to_broadcast([v.shape[0], n, v.shape[1]])

            def three(v, n):
                return v.rearrange("p (a n) -> p a n", n=n)

            def low(s, w=SL):
                for c in range(WC):
                    dve.wait_ge(w_hi, s * WC + (c + 1))
                    dve.sem_inc(t_dve, 1)
                    src = raw[:, s % 2, 2 * c:2 * c + 2, 0:w] if isinstance(s, int) else (
                        raw[:, bass.ds(s % 2, 1), 2 * c:2 * c + 2, 0:w].rearrange("p a k n -> p (a k) n"))
                    dve.tensor_tensor(wgt_l[:, 2 * c:2 * c + 2, 0:w], src, f(wgt_h[:, 2 * c:2 * c + 2, 0:w]),
                                    ALU.subtract).then_inc(w_lo, 1)

            def tile_low(t, h, q):
                dve.wait_ge(tp_hi, q)
                dve.sem_inc(t_dve, 1)
                dve.tensor_tensor(act_l[:, 4 * h:4 * h + 4, bass.ds(t * P, P)],
                                bank(2 + h).rearrange("p (k n) -> p k n", k=4),
                                f(act_h[:, 4 * h:4 * h + 4, bass.ds(t * P, P)]), ALU.subtract).then_inc(tp_lo, 1)

            with dve.Fori(0, NT // 2) as v:
                for j in range(2):
                    for h in range(2):
                        tile_low(v * 2 + j, h, v * 4 + (2 * j + h + 1))
            low(0)
            low(1)
            low(S_SKV)
            dve.wait_ge(bias_ld, 32)
            dve.tensor_copy(bias[:, 0, :], bias[:, 1, :]).then_inc(dve_own, 1)
            dve.wait_ge(dve_own, own.done())
            dve.memset(three(bias[:, 0, :], P)[:, :, 0:CHUNK], NEG).then_inc(dve_own, 1)
            dve.wait_ge(dve_own, own.done())
            low(S_GATE)

            dve.wait_ge(c_ld, CONSTS)
            with own.loop(dve, 4, 28) as i:
                for j in range(4):
                    n = i * 4 + j
                    dve.wait_ge(sc_done, n + 2)
                    dve.sem_inc(t_dve, 1)
                    b = bias[:, bass.ds((i + 3) // 4, 1), :].rearrange("p a n -> p (a n)") if j == 0 else bias[:, 1, :]
                    dve.tensor_tensor(sc_s, bank(4, 2), b, ALU.add).then_inc(dve_own, 1)
                    dve.wait_ge(dve_own, own.done())
                    dve.sem_inc(t_dve, 1)
                    dve.tensor_reduce(s_mx, three(sc_s, P), AX.X, ALU.max).then_inc(dve_own, 1)
                    dve.wait_ge(dve_own, own.done())
                    dve.sem_inc(t_dve, 1)
                    dve.tensor_tensor(s_mx, s_mx, sink, ALU.max).then_inc(dve_own, 1)
                    dve.wait_ge(dve_own, own.done())
                    dve.sem_inc(t_dve, 1)
                    dve.tensor_tensor(s_sd, sink, s_mx, ALU.subtract).then_inc(dve_own, 1)
                    dve.wait_ge(dve_own, own.done())
                    dve.sem_inc(t_dve, 1)
                    dve.tensor_tensor(three(sc_s, P), three(sc_s, P), over(s_mx, P), ALU.subtract).then_inc(mx_ok, 1)
                    dve.wait_ge(e_ok, n + 1)
                    dve.sem_inc(t_dve, 1)
                    dve.tensor_reduce(s_den, three(pr_s, P), AX.X, ALU.add).then_inc(dve_own, 1)
                    dve.wait_ge(dve_own, own.done())
                    dve.sem_inc(t_dve, 1)
                    dve.tensor_tensor(s_den, s_den, s_es, ALU.add).then_inc(dve_own, 1)
                    dve.wait_ge(dve_own, own.done())
                    dve.sem_inc(t_dve, 1)
                    dve.reciprocal(s_den, s_den).then_inc(dve_own, 1)
                    dve.wait_ge(dve_own, own.done())
                    dve.sem_inc(t_dve, 1)
                    dve.tensor_tensor(three(pr_s, P), three(pr_s, P), over(s_den, P), ALU.mult).then_inc(p_ok, 1)
                    if j == 3:
                        low(i + (S_GATE + 1))
                    if j % 2 == 0:
                        dve.wait_ge(ot_st, i * 32 + 16 * (j // 2 + 1))
                        dve.sem_inc(t_dve, 1)
                    dve.wait_ge(pv_done, n + 3)
                    dve.sem_inc(t_dve, 1)
                    dve.tensor_copy(oT_s[:, :, (j % 2) * CHUNK:(j % 2 + 1) * CHUNK], three(bank(6), CHUNK)
                                  ).then_inc(ot_ev, 1)
            low(S_LR, P)
            low(S_KV)
            with dve.Fori(0, 3) as i:
                low(i + (S_KV + 1))

            dve.wait_ge(gu_one, 2)
            dve.sem_inc(go_st, 16)
            dve.memset(st_b, 0.0).then_inc(dve_own, 1)
            dve.wait_ge(dve_own, own.done())
            with dve.Fori(0, NT // 2) as v:
                for j in range(2):
                    t = v * 2 + j
                    dve.wait_ge(gg_abs, t + 1)
                    dve.sem_inc(t_dve, 1)
                    dve.scalar_tensor_tensor(gla_l, bank(0), 0.0, gla_t, ALU.min, ALU.subtract).then_inc(gg_la, 1)
                    dve.wait_ge(gg_dec, t + 1)
                    dve.sem_inc(t_dve, 1)
                    dve.tensor_tensor(kdec, kvst[j][:, 0:SL], gla_t, ALU.mult).then_inc(gg_kd, 1)
                    for c, (new, old) in enumerate(((st_a, st_b), (st_b, st_a))):
                        dve.wait_ge(gu_mm, t * 2 + (c + 1))
                        dve.sem_inc(t_dve, 1)
                        for h in range(GH):
                            dve.scalar_tensor_tensor(new[:, h, :], old[:, h, :], gam[:, h, c:c + 1],
                                                   bank(2 + 2 * c, 2)[:, h * GV:(h + 1) * GV], ALU.mult, ALU.add
                                                   ).then_inc(gs_up, 1)
                        dve.wait_ge(gs_up, t * 8 + 4 * (c + 1))
                        dve.sem_inc(t_dve, 1)
                    dve.wait_ge(go_sq, t + 1)
                    dve.sem_inc(t_dve, 1)
                    dve.tensor_reduce(ssq[:, bass.ds(t, 1), :].rearrange("p a h -> p (a h)"), three(o_q, GV), AX.X, ALU.add)
                    dve.wait_ge(go_st, t * 16 + 16)
                    dve.sem_inc(t_dve, 1)
                    dve.tensor_copy(o_s, bank(6, 2)).then_inc(go_ev, 1)
            dve.wait_ge(go_ev, NT)
            dve.tensor_scalar(ssq, ssq, 1.0 / GV, EPS, ALU.mult, ALU.add).then_inc(rs_v, 1)
            dve.wait_ge(rs_s, 1)
            dve.reciprocal(ssq, ssq).then_inc(dve_own, 1)
            dve.wait_ge(dve_own, own.done())
            dve.wait_ge(gu_ld, 48)
            for i in range(NS):
                for t in range(NT):
                    if t == NT - 1:
                        low(S_R + 1 + i)
                    j, n = t % 2, i * (NT // 2) + t // 2
                    dve.wait_ge(o_ld[j], 16 * (n + 1))
                    dve.wait_ge(pj_free[j], B_R + n + 2)
                    if n:
                        dve.wait_ge(a_ok[j], n)
                    for h in range(2):
                        dve.scalar_tensor_tensor(rtmp[j][:, h * GV:(h + 1) * GV], opc[j][:, h * GV:(h + 1) * GV],
                                               ssq[:, t, 2 * i + h:2 * i + h + 1],
                                               rsil[j][:, h * GV:(h + 1) * GV], ALU.mult, ALU.mult).then_inc(dve_own, 1)
                        dve.wait_ge(dve_own, own.done())
                    if n:
                        dve.wait_ge(a_st[j], 16 * n)
                    dve.tensor_tensor(apc[j], rtmp[j], ng_bc[:, i * SL:(i + 1) * SL], ALU.mult).then_inc(a_ok[j], 1)
            with dve.Fori(0, NT // 2) as v:
                for j in range(2):
                    for h in range(2):
                        tile_low(v * 2 + j, h, v * 4 + (2 * NT + 2 * j + h + 1))

            for s, base, nb in ((S_WG, 0, B_WG), (S_WS, KC, B_WS)):
                for k in range(KC):
                    for h in range(2):
                        if k % CPS == CPS - 1 and h == 1:
                            low(s + 1 + k // CPS)
                        dve.wait_ge(gt_free[h], base + k + 1)
                        dve.wait_ge(pj_done[h], nb + k + 1)
                        m = mT[:, k, h * SL:(h + 1) * SL]
                        out = mtmp[h] if base else m
                        if base and k:
                            dve.wait_ge(m_ok, 2 * k + h - 1)
                        dve.tensor_tensor(out, bank(h), gsg[h], ALU.mult).then_inc(pj_free[h], 1)
                        if base:
                            dve.wait_ge(pj_free[h], nb + k + 2)
                            dve.tensor_tensor(m, m, mtmp[h], ALU.add).then_inc(m_ok, 1)
                for k in range(KC):
                    dve.wait_ge(tp_hi, 4 * NT + base + k + 1)
                    dve.tensor_tensor(act_l[:, k, :], mT[:, k, :] if base else nat[k % 2], f(act_h[:, k, :]),
                                    ALU.subtract).then_inc(tp_lo, 1)
            for i in range(NS):
                for t in range(NT):
                    if t == NT - 1:
                        low(S_WO + 1 + i, SL if i == 0 else NLOG)
                    j, n = t % 2, i * (NT // 2) + t // 2
                    dve.wait_ge(xp_ld[j], 16 * (n + 1))
                    dve.wait_ge(pj_done[j], B_WO + n + 1)
                    piece = y_n[:, t, i * SL:(i + 1) * SL]
                    dve.scalar_tensor_tensor(piece, xpc[j], ALPHA, bank(j), ALU.mult, ALU.add).then_inc(pj_free[j], 1)
                    dve.wait_ge(pj_free[j], B_WO + n + 2)
                    dve.bn_stats(stats[:, t, i, :], piece).then_inc(dve_own, 1)
                    dve.wait_ge(dve_own, own.done())
            for t in range(NT):
                dve.bn_aggr(mv[:, t, :], stats[:, t].rearrange("p i s -> p (i s)")).then_inc(dve_own, 1)
                dve.wait_ge(dve_own, own.done())
            dve.tensor_scalar(rstd, mv[:, :, 1], EPS, None, ALU.add).then_inc(ln_v, 1)
            dve.wait_ge(ln_s, 1)
            dve.reciprocal(rstd, rstd).then_inc(dve_own, 1)
            dve.wait_ge(dve_own, own.done())
            dve.scalar_tensor_tensor(nmr, mv[:, :, 0], -1.0, rstd, ALU.mult, ALU.mult).then_inc(ln_r, 1)
            dve.wait_ge(ln_ld, 32)
            for t in range(NT + 1):
                if t < NT:
                    j = t % 2
                    dve.wait_ge(xn_ok, t + 1)
                    dve.tensor_tensor(xn[j], xn[j], ln_g, ALU.mult).then_inc(dve_own, 1)
                    dve.wait_ge(dve_own, own.done())
                    if t > 1:
                        dve.wait_ge(tp_done, 4 + 4 * NT + 2 * (t - 1))
                        dve.wait_ge(x1_stored[j], 16 * (t // 2))
                    dve.tensor_tensor(nat[j], xn[j], ln_b, ALU.add).then_inc(x1_ready[j], 1)
                if t > 0:
                    for h in range(2):
                        tile_low(t - 1, h, 4 * NT + 2 * KC + 2 * (t - 1) + h + 1)
            low(S_PG)

            dve.wait_ge(lg_tp, 1)
            dve.wait_ge(pw_ld, 64)
            dve.tensor_tensor(lg, bank(2, 2).rearrange("p (t n) -> p t n", t=NT)[:, :, 0:NLOG],
                            along(rb_bc, NT), ALU.add).then_inc(dve_own, 1)
            dve.wait_ge(dve_own, own.done())
            lg_g = lg[:, :, 0:NG]
            i8 = cst[:, K_I8:K_I8 + EPG]

            def first_of(onehot, x, mx, n, scratch, ix):
                dve.tensor_reduce(mx, x, AX.X, ALU.max).then_inc(dve_own, 1)
                dve.wait_ge(dve_own, own.done())
                dve.tensor_tensor(scratch, x, over(mx, n), ALU.is_ge).then_inc(dve_own, 1)
                dve.wait_ge(dve_own, own.done())
                dve.tensor_tensor(scratch, scratch, along(i8[:, 0:n], NT), ALU.mult).then_inc(dve_own, 1)
                dve.wait_ge(dve_own, own.done())
                dve.tensor_reduce(ix, scratch, AX.X, ALU.min).then_inc(dve_own, 1)
                dve.wait_ge(dve_own, own.done())
                dve.tensor_tensor(onehot, along(i8[:, 0:n], NT), over(ix, n), ALU.is_equal).then_inc(dve_own, 1)
                dve.wait_ge(dve_own, own.done())
            first_of(g_oh, lg_g, g_mx, NG, g_e, g_ix)
            dve.tensor_tensor(g_e, lg_g, over(g_mx, NG), ALU.subtract).then_inc(r_mx, 1)
            e4 = e_all.rearrange("p t (g e) -> p t g e", g=NG)
            for g in range(NG):
                x = lg[:, :, NG + EPG * g:NG + EPG * (g + 1)]
                dve.tensor_tensor(e4[:, :, g, :], x, g_oh[:, :, g:g + 1].to_broadcast([P, NT, EPG]), ALU.mult).then_inc(dve_own, 1)
                dve.wait_ge(dve_own, own.done())
            dve.tensor_tensor(e_sel, e4[:, :, 0, :], e4[:, :, 1, :], ALU.add).then_inc(dve_own, 1)
            dve.wait_ge(dve_own, own.done())
            for g in range(2, NG):
                dve.tensor_tensor(e_sel, e_sel, e4[:, :, g, :], ALU.add).then_inc(dve_own, 1)
                dve.wait_ge(dve_own, own.done())
            first_of(e_oh[0], e_sel, e_mx[0], EPG, e_t, g_ix)
            dve.scalar_tensor_tensor(e_m, e_oh[0], NEG, e_sel, ALU.mult, ALU.add).then_inc(dve_own, 1)
            dve.wait_ge(dve_own, own.done())
            first_of(e_oh[1], e_m, e_mx[1], EPG, e_t, g_ix)
            dve.tensor_tensor(e_mx[1], e_mx[1], e_mx[0], ALU.subtract).then_inc(r_dif, 1)
            for c in range(2):
                o4 = oh[c].rearrange("p t (g e) -> p t g e", g=NG)
                for g in range(NG):
                    dve.tensor_tensor(o4[:, :, g, :], e_oh[c], g_oh[:, :, g:g + 1].to_broadcast([P, NT, EPG]),
                                    ALU.mult).then_inc(dve_own, 1)
                    dve.wait_ge(dve_own, own.done())
            dve.tensor_tensor(ohs, oh[0], oh[1], ALU.add).then_inc(r_oh, 1)
            dve.wait_ge(r_ex, 1)
            dve.tensor_reduce(g_sum, g_e, AX.X, ALU.add).then_inc(dve_own, 1)
            dve.wait_ge(dve_own, own.done())
            dve.wait_ge(r_e2, 1)
            dve.tensor_scalar(e_mx[0], e_mx[1], 1.0, None, ALU.add).then_inc(dve_own, 1)
            dve.wait_ge(dve_own, own.done())
            dve.tensor_tensor(e_mx[0], e_mx[0], g_sum, ALU.mult).then_inc(dve_own, 1)
            dve.wait_ge(dve_own, own.done())
            dve.reciprocal(slot_w[:, 0, :], e_mx[0]).then_inc(dve_own, 1)
            dve.wait_ge(dve_own, own.done())
            dve.tensor_tensor(slot_w[:, 1, :], slot_w[:, 0, :], e_mx[1], ALU.mult).then_inc(dve_own, 1)
            dve.wait_ge(dve_own, own.done())

            def place():
                dve.wait_ge(r_mm, 1)
                earlier = bank(6)[:, 0:NT * NE].rearrange("p (t e) -> p t e", t=NT)
                in_tile = bank(7)[:, 0:NT * NE].rearrange("p (t e) -> p t e", t=NT)
                dve.memset(pre[:, 0, :], 0.0).then_inc(dve_own, 1)
                dve.wait_ge(dve_own, own.done())
                for t in range(1, NT):
                    dve.tensor_tensor(pre[:, t, :], pre[:, t - 1, :], in_tile[:, t - 1, :], ALU.add).then_inc(dve_own, 1)
                    dve.wait_ge(dve_own, own.done())
                dve.tensor_tensor(cnt, pre[:, NT - 1, :], in_tile[:, NT - 1, :], ALU.add).then_inc(dve_own, 1)
                dve.wait_ge(dve_own, own.done())
                dve.tensor_tensor(rank, pre, earlier, ALU.add).then_inc(dve_own, 1)
                dve.wait_ge(dve_own, own.done())
                dve.tensor_scalar(nbk, cnt, 0.0, None, ALU.is_gt).then_inc(dve_own, 1)
                dve.wait_ge(dve_own, own.done())
                for m in range(1, SEQ // P):
                    dve.scalar_tensor_tensor(nbk, cnt, float(P * m), nbk, ALU.is_gt, ALU.add).then_inc(dve_own, 1)
                    dve.wait_ge(dve_own, own.done())
                x, y = btmp, bend
                dve.tensor_copy(x, nbk).then_inc(dve_own, 1)
                dve.wait_ge(dve_own, own.done())
                for sh in (1, 2, 4, 8, 16):
                    dve.tensor_copy(y[:, 0:sh], x[:, 0:sh]).then_inc(dve_own, 1)
                    dve.wait_ge(dve_own, own.done())
                    dve.tensor_tensor(y[:, sh:NE], x[:, sh:NE], x[:, 0:NE - sh], ALU.add).then_inc(dve_own, 1)
                    dve.wait_ge(dve_own, own.done())
                    x, y = y, x
                dve.tensor_tensor(nbk, x, nbk, ALU.subtract).then_inc(dve_own, 1)
                dve.wait_ge(dve_own, own.done())
                dve.tensor_scalar(nbk, nbk, float(P), None, ALU.mult).then_inc(dve_own, 1)
                dve.wait_ge(dve_own, own.done())
                dve.tensor_tensor(rank, rank, along(nbk, NT), ALU.add).then_inc(dve_own, 1)
                dve.wait_ge(dve_own, own.done())
                for c in range(2):
                    dve.tensor_tensor(rt, oh[c], rank, ALU.mult).then_inc(dve_own, 1)
                    dve.wait_ge(dve_own, own.done())
                    dve.tensor_reduce(slot_f, rt, AX.X, ALU.add).then_inc(dve_own, 1)
                    dve.wait_ge(dve_own, own.done())
                    dve.tensor_copy(slot_i[:, c, :], slot_f).then_inc(slots_ok, 1)
                dve.tensor_scalar(nb_i, x[:, NE - 1:NE], float(-MINB), None, ALU.add).then_inc(dve_own, 1)
                dve.wait_ge(dve_own, own.done())
                dve.tensor_tensor(be_cmp, along(x[0:1, :], MAXB), over(cst[0:1, K_I48:K_I48 + MAXB], NE), ALU.is_le).then_inc(dve_own, 1)
                dve.wait_ge(dve_own, own.done())
                dve.tensor_reduce(be_f, be_cmp, AX.X, ALU.add).then_inc(dve_own, 1)
                dve.wait_ge(dve_own, own.done())
                dve.tensor_copy(be_row, be_f).then_inc(nb_ok, 1)

            for i in range(NS):
                for t in range(NT):
                    j, n = t % 2, i * (NT // 2) + t // 2
                    dve.wait_ge(pj_done[j], B_PG + n + 1)
                    dve.tensor_tensor(gpre[j], bank(j), pg_bc[:, i * SL:(i + 1) * SL], ALU.add).then_inc(pj_free[j], 1)
                    if i == 0 and t == NT - 1:
                        low(S_PG + 1)
                    dve.wait_ge(gs_ok[j], n + 1)
                    dve.wait_ge(pp_done[j], n + 1)
                    if n:
                        dve.wait_ge(z2_ok[j], n)
                    dve.tensor_tensor(ptmp[j], bank(4 + j), gpre[j], ALU.mult).then_inc(pp_free[j], 1)
                    dve.wait_ge(pp_free[j], n + 2)
                    dve.wait_ge(x1_ld[j], 16 * (n + 1))
                    if n:
                        dve.wait_ge(z2_st[j], 16 * n)
                    dve.scalar_tensor_tensor(z2p[j], x1p[j], ALPHA, ptmp[j], ALU.mult, ALU.add).then_inc(z2_ok[j], 1)
                if i == 0:
                    place()

            dve.wait_ge(nb_ok, 1)
            last_b = dve.snap(dve.value_load(nb_i[0:1, 0:1], min_val=0, max_val=MAXB - MINB) + (MINB - 1))

            def low_expert(m, b, dst, high, src):
                w = dst.shape[1] // WC
                for c in range(WC):
                    dve.wait_ge(m_hi[m], b * WC + (c + 1))
                    dve.sem_inc(t_dve, 1)
                    dve.tensor_tensor(dst[:, w * c:w * (c + 1), :], arrived(src, m, b, slice(w * c, w * (c + 1))),
                                    f(high[:, w * c:w * (c + 1), :]), ALU.subtract).then_inc(m_lo[m], 1)

            def x_low(b):
                for h in range(2):
                    dve.wait_ge(xt_hi, b * 2 + (h + 1))
                    dve.sem_inc(t_dve, 1)
                    dve.tensor_tensor(blk_l[:, 4 * h:4 * h + 4, :], bank(2 + h).rearrange("p (k n) -> p k n", k=4),
                                    f(blk_h[:, 4 * h:4 * h + 4, :]), ALU.subtract).then_inc(xt_lo, 1)

            def block_step(b, first, last):
                if not last:
                    low_expert(0, b + 1, wgt_l, wgt_h, ring_up)
                    low_expert(1, b + 1, u_l, u_h, ring_up)
                dve.wait_ge(sl_ok, b + 1)
                dve.sem_inc(t_dve, 1)
                dve.wait_ge(um_done, b + 1)
                dve.sem_inc(t_dve, 1)
                if not first:
                    dve.wait_ge(ht_done, b)
                    dve.sem_inc(t_dve, 1)
                dve.tensor_tensor(hid, bank(1), sig, ALU.mult).then_inc(h_ok, 1)
                if not last:
                    x_low(b + 1)
                low_expert(2, b, d_l, d_h, ring_down)
                dve.wait_ge(ht_hi, b + 1)
                dve.sem_inc(t_dve, 1)
                dve.tensor_tensor(blk_l[:, KC:KC + FC, :], bank(4).rearrange("p (k n) -> p k n", k=FC),
                                f(blk_h[:, KC:KC + FC, :]), ALU.subtract).then_inc(ht_lo, 1)
            x_low(0)
            low_expert(0, 0, wgt_l, wgt_h, ring_up)
            low_expert(1, 0, u_l, u_h, ring_up)
            block_step(0, True, False)
            with dve.Fori(1, last_b) as b:
                block_step(b, False, False)
            block_step(last_b, False, True)

            dve.wait_ge(z_ld, 16 * NT)
            for t in range(NT):
                j = t % 2
                dve.wait_ge(f_z[t % (NT // 2)], 32 * (t // (NT // 2) + 1))
                for c, y in enumerate((y0, y1)):
                    dve.scalar_tensor_tensor(zt[t], y[t % (NT // 2)], slot_w[:, c, t:t + 1], zt[t],
                                             ALU.mult, ALU.add).then_inc(dve_own, 1)
                    dve.wait_ge(dve_own, own.done())
                for i in range(NS):
                    dve.bn_stats(fst[:, j, i, :], zt[t][:, i * SL:(i + 1) * SL]).then_inc(dve_own, 1)
                    dve.wait_ge(dve_own, own.done())
                dve.bn_aggr(fmv[:, j, :], fst[:, j].rearrange("p i s -> p (i s)")).then_inc(dve_own, 1)
                dve.wait_ge(dve_own, own.done())
                if t > 1:
                    dve.wait_ge(f_n, t - 1)
                dve.tensor_scalar(frs[:, j, :], fmv[:, j, 1:2], EPS, None, ALU.add).then_inc(f_var, 1)
                dve.wait_ge(f_sq, t + 1)
                dve.reciprocal(frs[:, j, :], frs[:, j, :]).then_inc(dve_own, 1)
                dve.wait_ge(dve_own, own.done())
                dve.scalar_tensor_tensor(fnm[:, j, :], fmv[:, j, 0:1], -1.0, frs[:, j, :], ALU.mult, ALU.mult
                                         ).then_inc(f_rs, 1)


_INS = ["x", "p", "rel_table", "w_in", "gla_gate_up", "gla_gate_b", "gla_norm_g", "swa_sinks",
        "branch_gate_b", "w_branch_gla", "w_branch_swa", "w_out", "ln1_g", "ln1_b",
        "router_group_w", "router_group_b", "router_expert_w", "router_expert_b",
        "expert_w_gate", "expert_w_up", "expert_w_down", "w_ple", "w_ple_gate", "ple_gate_b",
        "ln2_g", "ln2_b"]


def shape_constants():
    i = np.arange(P)
    cst = np.zeros((P, K_ALL), np.float32)
    cst[:, K_ID:K_ID + P] = np.eye(P)
    cst[:, K_SUF:K_SUF + P] = (i[:, None] > i[None, :]) & (i[:, None] // CHUNK == i[None, :] // CHUNK)
    cst[:, K_ERL:K_ERL + P] = i[:, None] < i[None, :]
    cst[:, K_ONE:K_ONE + P] = 1
    cst[:, K_CH:K_CH + 2] = i[:, None] // CHUNK == np.arange(2)[None, :]
    cst[:, K_I8:K_I8 + EPG] = np.arange(EPG) - EPG
    cst[:, K_I48:K_I48 + MAXB] = np.arange(MAXB)
    tok = i[:, None] + P * np.arange(NT)[None, :]
    toki = np.stack([np.stack([tok, c * SEQ + tok], -1) for c in range(2)], 1).astype(np.int32)
    s = np.arange(MAXB * P)
    empty = np.stack([0 * s, 2 * SEQ + s % P], 1).astype(np.int32)
    rel = np.arange(REL) - (P - 1)
    half, exact = 16, 8
    n = np.abs(rel)
    large = exact + (np.log(np.maximum(n, 1) / exact) / np.log(128 / exact) * (half - exact)).astype(np.int32)
    b = (rel > 0) * half + np.where(n < exact, n, np.minimum(large, half - 1))
    bucket = (np.arange(2 * half)[:, None] == b[None, :]).astype(np.float32)
    return {"cst": cst, "toki": toki, "bucket": bucket, "empty": empty}


def kernel(**inputs):
    import concourse.bacc as _bacc
    from concourse.bass_utils import run_bass_kernel_spmd as _run

    nc = _bacc.Bacc("TRN2", target_bir_lowering=False, num_devices=1)
    given = {k: np.ascontiguousarray(inputs[k]) for k in _INS}
    given.update(shape_constants())
    a = {k: nc.dram_tensor(f"in_{k}", v.shape, mybir.dt.from_np(v.dtype), kind="ExternalInput").ap()
         for k, v in given.items()}
    a["out"] = nc.dram_tensor("out_0", (1, SEQ, D), F32, kind="ExternalOutput").ap()
    build(nc, a)
    r = _run(nc, [{f"in_{k}": v for k, v in given.items()}], core_ids=[0])
    return r.results[0]["out_0"]
```

```python
from contextlib import ExitStack, contextmanager

import numpy as np

import concourse.bass as bass
from concourse import mybir
from concourse.alu_op_type import AluOpType as ALU

ACT = mybir.ActivationFunctionType
AX = mybir.AxisListType
F32 = mybir.dt.float32
F32R = mybir.dt.float32r
I32 = mybir.dt.int32

P = 128
D = 1024
SEQ = 1024
NT = SEQ // P
KC = D // P
CHUNK = 64
ALPHA = 2.0 ** 0.25
EPS = 1e-5
SL = 512
NS = D // SL
CPS = SL // P
WC = KC // 2

GH, GK, GV, RANK, TAU = 4, 128, 256, 16, 16.0
HEADS, KVH, HD = 16, 4, 64
PAIRS = HEADS // 2
REL = 191
NEG = -1e30

NG, EPG, NE = 4, 8, 32
DE = 512
FC = DE // P
MAXB = 48
MINB = 16
RING = 5
NLOG = NG + NE
PLE = 256
PKC = PLE // P

C_GQ, C_GK, C_LR, C_R, C_SQ, C_SK, C_GA = 0, 512, 2048, 2064, 3088, 4112, 4624

S_SQ, S_SKV, S_GATE, S_KV, S_LR, S_GQ, S_R, S_WG, S_WS, S_WO, S_RT, S_PG, S_END = (
    0, 2, 3, 7, 10, 11, 12, 14, 16, 18, 20, 21, 23)
B_SQ, B_SK, B_SV, B_GATE, B_KV, B_LR, B_GQ, B_R, B_WG, B_WS, B_WO, B_RT, B_PG = (
    0, 8, 10, 14, 30, 42, 43, 47, 55, 63, 71, 79, 80)
Z_SQ, Z_GATE, Z_GQ, Z_ALL = 0, 8, 24, 28
E_SQ, E_SV, E_GATE, E_KV, E_LR, E_GQ, E_END = 0, 8, 12, 28, 40, 41, 45

K_ID, K_SUF, K_ERL, K_ONE, K_CH, K_I8, K_I48, K_ALL = 0, 128, 256, 384, 512, 514, 522, 570
ARENA = 24900
CONSTS = 6 * 16
TL_X = 4 + 2 * NT
TL_A = TL_X + 2 * NT
TL_B = TL_A + KC
TL_M = TL_B + 2 * KC
TL_X1 = TL_M + 2 * NT


class Steps:

    def __init__(self):
        self.total, self.at = 0, 0
        self.i = self.per = None

    @contextmanager
    def loop(self, engine, n, per):
        with engine.Fori(0, n) as i:
            self.i, self.per, self.at = i, per, 0
            yield i
        assert self.at == per, (self.at, per)
        self.total += n * per
        self.i = None

    def done(self):
        if self.i is None:
            self.total += 1
            return self.total
        self.at += 1
        return self.i * self.per + (self.total + self.at)


def build(nc, a):
    ctx = ExitStack()
    with ctx:
        def dram(name, shape, dt=F32):
            return nc.dram_tensor(name, shape, dt, kind="Internal").ap()

        def sem(name):
            return ctx.enter_context(nc.semaphore(name))

        def sems(name, n):
            return [sem(f"{name}{i}") for i in range(n)]

        def sbuf(name, shape, dt=F32):
            return ctx.enter_context(nc.sbuf_tensor(name, shape, dt))

        z_d = dram("z_t", [Z_ALL, P, SEQ])
        rel_d = dram("rel_v", [HEADS, CHUNK, REL])
        sv_d = dram("sv_n", [CHUNK + SEQ, KVH * HD])
        lr_d = dram("lr_t", [RANK, SEQ])
        kv_d = dram("kv_n", [SEQ, 3 * SL])
        o_d = dram("o_n", [SEQ, D])
        b_d = dram("b_t", [PAIRS, P, SEQ])
        a_d = dram("a_n", [SEQ, D])
        x1_d = dram("x1_n", [SEQ, D])
        z2_d = dram("z2_n", [SEQ, D])
        slot_d = dram("slot_tok", [MAXB * P, 2], I32)
        y_d = dram("y_n", [2 * SEQ + P, D])

        act_h = sbuf("act_h", [P, KC, SEQ], F32R)
        act_l = sbuf("act_l", [P, KC, SEQ], F32R)
        wgt_h = sbuf("wgt_h", [P, KC, SL], F32R)
        wgt_l = sbuf("wgt_l", [P, KC, SL], F32R)
        blk_h = sbuf("blk_h", [P, KC + FC, P], F32R)
        blk_l = sbuf("blk_l", [P, KC + FC, P], F32R)
        cst = sbuf("cst", [P, K_ALL])
        toki = sbuf("toki", [P, 2, NT, 2], I32)
        arena = sbuf("arena", [P, ARENA])
        ident = cst[:, K_ID:K_ID + P]

        KEEP = ARENA - 192

        def region(at):
            end = ARENA if at == KEEP else KEEP
            mark = [at]

            def take(*shape, rows=P, dt=F32):
                n = int(np.prod(shape))
                assert mark[0] + n <= end, mark[0] + n
                v = arena[0:rows, mark[0]:mark[0] + n]
                mark[0] += n
                if dt != F32:
                    v = v.bitcast(dt)
                names = "abcd"[:len(shape)]
                if len(shape) > 1:
                    v = v.rearrange(f"p ({' '.join(names)}) -> p {' '.join(names)}",
                                    **{c: s for c, s in zip(names[:-1], shape)})
                return v
            return take

        SLOT = KC * SL
        raw = arena[:, 0:2 * SLOT].rearrange("p (s k n) -> p s k n", s=2, k=KC)
        take = region(2 * SLOT)
        ev = [take(SL) for _ in range(2)]
        AREA = 2 * SLOT + 2 * SL
        keep = region(KEEP)
        slot_i = keep(2, NT, dt=I32)
        slot_w = keep(2, NT)
        be_row = keep(MAXB, rows=1, dt=I32)
        nb_i = keep(1, dt=I32)
        idx, idy = keep(1, dt=I32), keep(1, dt=I32)
        slots = keep(MAXB, 2, dt=I32)

        take = region(AREA)
        kT = take(KVH, CHUNK + SEQ)
        bias = take(2, PAIRS * P)
        sc_s = take(PAIRS * P)
        pr_s = take(PAIRS * P)
        pT_s = take(PAIRS * P)
        qst = [take(PAIRS, P) for _ in range(2)]
        kst = take(KVH, P)
        vst = [take(KVH * HD) for _ in range(2)]
        oT_s = take(PAIRS, P)
        sink = take(PAIRS)
        gbias = take(2 * KC)
        s_mx, s_sd, s_es, s_den = (take(PAIRS) for _ in range(4))
        relt = oT_s[0:32, 0, 0:HEADS]
        buck = qst[0][0:32, 0:2, :].rearrange("p a b -> p (a b)")[:, 0:REL]
        relv = qst[1][0:HEADS, 0:2, :].rearrange("p a b -> p (a b)")[:, 0:REL]
        x_nat = [kT[:, g, CHUNK:CHUNK + D] for g in range(KVH)] + [pr_s, pT_s, sc_s, bias[:, 0, :]]

        take = region(AREA)
        kvst = [take(3 * SL) for _ in range(2)]
        lrst = [take(P, rows=32) for _ in range(2)]
        gqst = [take(GH, P) for _ in range(2)]
        gup = take(GH * GK, rows=32)
        gla_l, kdec = take(SL), take(SL)
        gla_t = [take(SL) for _ in range(2)]
        st_a, st_b = take(GH, GV), take(GH, GV)
        o_s, o_q = take(GH * GV), take(GH * GV)
        gam = [take(GH, 2) for _ in range(2)]
        ssq = take(NT, GH)
        rsil = [take(SL) for _ in range(2)]
        opc = [take(SL) for _ in range(2)]
        apc = [take(SL) for _ in range(2)]
        rtmp = [take(SL) for _ in range(2)]
        ng_bc = kvst[1][:, SL:3 * SL]

        take = region(AREA)
        nat = [take(D) for _ in range(2)]
        gld = [take(SL) for _ in range(2)]
        gsg = [take(SL) for _ in range(2)]
        mtmp = [take(SL) for _ in range(2)]
        mT = take(KC, SEQ)
        bst = nat + [take(D) for _ in range(2)]
        take = region(AREA + 2 * D)
        xpc = [take(SL) for _ in range(2)]
        stats = take(NT, NS, 6)
        mv = take(NT, 2)
        rstd, nmr = take(NT), take(NT)
        ln_g, ln_b = take(D), take(D)
        xn = [take(D) for _ in range(2)]
        y_n = take(NT, D)

        take = region(AREA + 2 * D)
        lgT = take(SEQ)
        pnat = [take(PLE) for _ in range(2)]
        pT = take(PKC, SEQ)
        wple = take(PKC, D)
        pg_bc = take(D)
        gpre = [take(SL) for _ in range(2)]
        ptmp = [take(SL) for _ in range(2)]
        z2p = [take(SL) for _ in range(2)]
        x1p = [take(SL) for _ in range(2)]
        rb_bc = take(NLOG)
        lg = take(NT, NLOG)
        g_mx, g_ix, g_sum = take(NT), take(NT), take(NT)
        g_e, g_oh = take(NT, NG), take(NT, NG)
        e_all = take(NT, NE)
        e_sel, e_t, e_m = take(NT, EPG), take(NT, EPG), take(NT, EPG)
        e_oh = [take(NT, EPG) for _ in range(2)]
        e_mx = [take(NT) for _ in range(2)]
        oh = [take(NT, NE) for _ in range(2)]
        ohs = take(NT, NE)
        rank, pre, rt = take(NT, NE), take(NT, NE), take(NT, NE)
        cnt, nbk, bend, btmp = take(NE), take(NE), take(NE), take(NE)
        slot_f = take(NT)
        take = region(AREA)
        be_cmp = take(MAXB, NE, rows=1)
        be_f = take(MAXB, rows=1)

        u_h = act_h[:, 0:4, :].rearrange("p a b -> p (a b)").rearrange("p (k n) -> p k n", k=KC)
        u_l = act_l[:, 0:4, :].rearrange("p a b -> p (a b)").rearrange("p (k n) -> p k n", k=KC)
        d_h, d_l = act_h[:, 4:8, :], act_l[:, 4:8, :]
        ring = arena[:, 0:RING * SLOT]
        ring_up = ring.rearrange("p (r k n) -> p r k n", r=RING, k=KC)
        ring_down = ring.rearrange("p (r k n) -> p r k n", r=RING, k=FC)
        take = region(RING * SLOT)
        sig = take(SL)
        hid = take(SL)
        y_s = take(D)
        xb = take(D)
        take = region(0)
        zt = [take(D) for _ in range(NT)]
        assert NT * D <= 2 * SLOT
        l2g, l2b = take(D), take(D)
        y0 = [take(D) for _ in range(NT // 2)]
        y1 = [take(D) for _ in range(NT // 2)]
        assert (NT + 2 + NT) * D <= RING * SLOT
        zn = [take(D) for _ in range(2)]
        zo = [take(D) for _ in range(2)]
        fst, fmv = take(2, 2, 6), take(2, 2)
        frs, fnm = take(2, 1), take(2, 1)

        ps = ctx.enter_context(nc.psum_tensor("ps", [P, 8, SL], F32))

        cst_ld, c_ld = sem("cst_loaded"), sem("constants_loaded")
        w_loaded, w_hi, w_lo, w_used = sem("w_loaded"), sem("w_hi"), sem("w_lo"), sem("w_used")
        n_loaded = sems("nat_loaded", 2)
        x1_ready = sems("x1_ready", 2)
        x1_stored = sems("x1_stored", 2)
        tp_done, tp_hi, tp_lo = sem("tp_done"), sem("tp_hi"), sem("tp_lo")
        pj_done, pj_free = sems("pj_done", 2), sems("pj_free", 2)
        ev_stored = sems("ev_stored", 2)
        rel_mm, rel_ev, rel_st, bias_ld = (
            sem(n) for n in ("rel_mm", "rel_ev", "rel_st", "bias_ld"))
        kt_pad = sem("kt_pad")
        q_ld, v_ld = sems("q_ld", 2), sems("v_ld", 2)
        k_st, sc_done, mx_ok, e_ok, p_ok, pt_done, pt_ev, pv_done, ot_ev, ot_st = (
            sem(n) for n in ("k_staged", "scores_done", "max_ok", "exp_ok", "probs_ok", "pt_done",
                             "pt_evacuated", "pv_done", "ot_evacuated", "ot_stored"))
        gu_ld, gu_one = sem("gate_up_norm_ld"), sem("gate_up_one")
        g_ld, gq_ld = sems("gla_ld", 2), sems("gla_q_ld", 2)
        gg_mm, gg_abs, gg_la, gg_suf, gg_dec, gg_kd, gu_mm, gs_up, go_mm, go_sq, go_ev, go_st = (
            sem(n) for n in ("glog_mm", "glog_ev", "glog_ok", "suffix_mm", "decay_ok", "kdec_ok",
                             "update_mm", "state_ok", "o_mm", "o_squared", "o_evacuated", "o_stored"))
        o_ld, a_ok, rs_v, rs_s = (
            sems("o_ld", 2), sems("a_ok", 2), sem("rs_var"), sem("rs_sqrt"))
        a_st = sems("a_stored", 2)
        gt_ld, gt_free = sems("gate_ld", 2), sems("gate_ready", 2)
        b_ld, m_ok = sems("x_b_ld", 4), sem("merged_ok")
        x_ld = b_ld + n_loaded + o_ld
        xp_ld = sems("x_piece_ld", 2)
        ln_ld, ln_v, ln_s, ln_r, xn_ok = (
            sem("ln1_ld"), sem("ln1_var"), sem("ln1_sqrt"), sem("ln1_rstd"), sem("xn_ok"))
        p_ld, p_tp, p_ev, pw_ld = sems("p_ld", 2), sem("p_tp"), sem("p_ev"), sem("ple_w_ld")
        lg_tp, r_mx, r_ex, r_dif, r_e2, r_oh, r_mm = (
            sem(n) for n in ("lg_tp", "r_max", "r_exp", "r_dif", "r_e2", "r_onehot", "r_mm"))
        zs_st, slots_ok, scat, nb_ok = (
            sem(n) for n in ("slots_empty", "slots_ok", "scattered", "blocks_ok"))
        pp_done, pp_free = sems("pp_done", 2), sems("pp_free", 2)
        gs_ok, z2_ok = sems("gsig_ok", 2), sems("z2_ok", 2)
        z2_st = sems("z2_st", 2)
        m_ld, m_hi, m_lo, m_used = sems("moe_ld", 3), sems("moe_hi", 3), sems("moe_lo", 3), sems("moe_used", 3)
        idx_ok, xb_ld, xt_done, xt_hi, xt_lo = (
            sem(n) for n in ("idx_ok", "xb_ld", "xt_done", "xt_hi", "xt_lo"))
        gm_done, um_done, sl_ok, h_ok, ht_done, ht_hi, ht_lo, y_done, y_ev, y_st = (
            sem(n) for n in ("gate_done", "up_done", "silu_ok", "h_ok", "ht_done", "ht_hi", "ht_lo",
                             "y_done", "y_evacuated", "slots_y_stored"))
        l2_ld, z_ld, f_g, f_z = sem("ln2_ld"), sem("z2_ld"), sem("f_gained"), sems("y_ld", NT // 2)
        f_var, f_sq, f_rs, f_n, f_o = sem("f_var"), sem("f_sqrt"), sem("f_rstd"), sem("f_normed"), sems("f_out", 2)
        f_st = sems("f_stored", 2)
        t_sp, t_act, t_pe, t_dve, t_pool = (sem(f"tick_{n}") for n in ("sp", "act", "pe", "dve", "pool"))
        act_own, dve_own = sem("act_own"), sem("dve_own")

        w_in = a["w_in"][0]

        def cols(w, c, n=SL):
            return w[:, bass.ds(c, n)].rearrange("(k p) n -> p k n", p=P)

        def bcast(v, n):
            return bass.AP(tensor=v.tensor, offset=v.offset, ap=[[0, P], [1, n]])

        def bank(b, n=1):
            return ps[:, b:b + n, :].rearrange("p a n -> p (a n)")

        def arrived(view, m, b, chunks):
            return view[:, bass.ds((b * 3 + m) % RING, 1), chunks, :].rearrange("p a k n -> p (a k) n")

        def f(v):
            return v.bitcast(F32)

        block = ctx.enter_context(nc.Block())

        def loaded(s):
            return s * 16 + (16 if not isinstance(s, int) or s < S_RT else 16 * (1 + NG))

        @block.sync
        def _(sp):
            def slot_free(s):
                if not isinstance(s, int) or s > 0:
                    sp.wait_ge(w_loaded, loaded(s - 1))
                    sp.sem_inc(t_sp, 1)
                if not isinstance(s, int) or s > 1:
                    sp.wait_ge(w_lo, s * WC - WC)
                    sp.sem_inc(t_sp, 1)

            def load_slice(s, src, n=SL):
                slot_free(s)
                dst = raw[:, s % 2, :, 0:n] if isinstance(s, int) else (
                    raw[:, bass.ds(s % 2, 1), :, 0:n].rearrange("p a k n -> p (a k) n"))
                sp.dma_start(dst, src).then_inc(w_loaded, 16)

            def tile(x, t, n=D):
                return x[bass.ds(t * P, P), 0:n]

            x = a["x"][0]
            sp.dma_start(cst[:, :], a["cst"]).then_inc(cst_ld, 16)
            for t in range(NT):
                sp.dma_start(x_nat[t], tile(x, t)).then_inc(x_ld[t], 16)
            load_slice(0, cols(w_in, C_SQ))
            load_slice(1, cols(w_in, C_SQ + SL))
            sp.dma_start(toki[:, :], a["toki"]).then_inc(c_ld, 16)
            sp.dma_start(slot_d, a["empty"]).then_inc(zs_st, 16)
            sp.dma_start(relt, a["rel_table"]).then_inc(c_ld, 16)
            sp.dma_start(buck, a["bucket"]).then_inc(c_ld, 16)
            with nc.allow_non_contiguous_dma(reason="a value for each channel or head on its partition"):
                sp.dma_start(gbias, a["branch_gate_b"].rearrange("l t (c p) -> p (l t c)", p=P)).then_inc(c_ld, 16)
                for r in range(2):
                    s0 = a["swa_sinks"]
                    sp.dma_start(sink[CHUNK * r:CHUNK * (r + 1), :],
                                 bass.AP(tensor=s0.tensor, offset=s0.offset + r, ap=[[0, CHUNK], [2, PAIRS]])
                                 ).then_inc(c_ld, 16)
            load_slice(S_SKV, cols(w_in, C_SK))
            load_slice(S_GATE, cols(w_in, C_GA))
            sp.wait_ge(rel_st, 16)
            for r in range(2):
                sp.dma_start(bias[CHUNK * r:CHUNK * (r + 1), 1, :].rearrange("p (h k) -> p h k", h=PAIRS),
                             bass.AP(tensor=rel_d.tensor, offset=r * CHUNK * REL + CHUNK - 1,
                                     ap=[[REL - 1, CHUNK], [2 * CHUNK * REL, PAIRS], [1, P]])).then_inc(bias_ld, 16)
            with sp.Fori(1, 4) as i:
                load_slice(i + S_GATE, cols(w_in, i * SL + C_GA))
            with sp.Fori(0, 3) as i:
                load_slice(i + S_KV, cols(w_in, i * SL + C_GK))
            load_slice(S_LR, cols(w_in, C_LR, P), P)
            load_slice(S_GQ, cols(w_in, C_GQ))
            load_slice(S_R, cols(w_in, C_R))

            sp.wait_ge(gu_one, 2)
            sp.dma_start(gup[0:RANK, :], a["gla_gate_up"][0]).then_inc(gu_ld, 16)
            sp.dma_start(gup[RANK:RANK + 1, :], a["gla_gate_b"]).then_inc(gu_ld, 16)
            for h in range(2):
                sp.wait_ge(ev_stored[h], 16 * E_GQ)

            def gla_load_kv(t, j):
                sp.dma_start(kvst[j], kv_d[bass.ds(t * P, P), :]).then_inc(g_ld[j], 16)
                sp.dma_start(lrst[j][0:RANK, :], lr_d[:, bass.ds(t * P, P)]).then_inc(g_ld[j], 16)

            def gla_load_q(t, j):
                sp.dma_start(gqst[j], z_d[Z_GQ:Z_GQ + GH, :, bass.ds(t * P, P)].rearrange("h p n -> p h n")
                             ).then_inc(gq_ld[j], 16)

            def gla_store(t):
                sp.wait_ge(go_ev, t + 2)
                sp.sem_inc(t_sp, 1)
                sp.dma_start(o_d[bass.ds(t * P, P), :], o_s).then_inc(go_st, 16)
            for j in range(2):
                gla_load_kv(j, j)
            load_slice(S_R + 1, cols(w_in, SL + C_R))
            for h in range(2):
                sp.wait_ge(ev_stored[h], 16 * E_END)
            for j in range(2):
                gla_load_q(j, j)
            load_slice(S_WG, cols(a["w_branch_gla"][0], 0))
            with sp.Fori(0, NT // 2 - 1) as v:
                for j in range(2):
                    t = v * 2 + j
                    sp.wait_ge(gu_mm, t * 2 + 2)
                    sp.sem_inc(t_sp, 1)
                    gla_load_kv(t + 2, j)
                    sp.wait_ge(go_mm, t + 1)
                    sp.sem_inc(t_sp, 1)
                    gla_load_q(t + 2, j)
                    gla_store(t)
            for t in range(NT - 2, NT):
                gla_store(t)
            sp.dma_start(ng_bc, bcast(a["gla_norm_g"], D)).then_inc(gu_ld, 16)
            sp.wait_ge(go_st, 16 * (NT + 1))
            def load_a(t):
                sp.wait_ge(a_st[t % 2], 16 * (NT // 2 + t // 2 + 1))
                if t > 1:
                    sp.wait_ge(tp_done, 4 + 2 * NT + 2 * (t - 1))
                sp.dma_start(nat[t % 2], tile(a_d, t)).then_inc(n_loaded[t % 2], 16)

            for i in range(NS):
                for t in range(NT):
                    k = i * (NT // 2) + t // 2
                    if k:
                        sp.wait_ge(a_ok[t % 2], k)
                    sp.dma_start(opc[t % 2], o_d[t * P:(t + 1) * P, i * SL:(i + 1) * SL]).then_inc(o_ld[t % 2], 16)
                    if i == NS - 1 and t > 2:
                        load_a(t - 3)
            for t in range(NT - 3, NT):
                load_a(t)

            def gates(base, src, s):
                for i in range(NS):
                    for c in range(CPS):
                        for h in range(2):
                            k = base + i * CPS + c
                            if k:
                                sp.wait_ge(gt_free[h], k)
                            sp.dma_start(gld[h], z_d[Z_GATE + k, :, h * SL:(h + 1) * SL]).then_inc(gt_ld[h], 16)
                    if i == 0:
                        load_slice(s, src)
            gates(0, cols(a["w_branch_gla"][0], SL), S_WG + 1)
            load_slice(S_WS, cols(a["w_branch_swa"][0], 0))
            for c in range(KC):
                sp.wait_ge(tp_lo, TL_A + max(c - 3, 0))
                sp.dma_start(bst[c % 4], b_d[c]).then_inc(b_ld[c % 4], 16)
            gates(KC, cols(a["w_branch_swa"][0], SL), S_WS + 1)
            load_slice(S_WO, cols(a["w_out"][0], 0))
            sp.wait_ge(tp_lo, TL_M)
            sp.dma_start(ln_g, bcast(a["ln1_g"], D)).then_inc(ln_ld, 16)
            sp.dma_start(ln_b, bcast(a["ln1_b"], D)).then_inc(ln_ld, 16)
            for i in range(NS):
                for t in range(NT):
                    k = i * (NT // 2) + t // 2
                    if k:
                        sp.wait_ge(pj_free[t % 2], B_WO + k + 1)
                    sp.dma_start(xpc[t % 2], x[t * P:(t + 1) * P, i * SL:(i + 1) * SL]).then_inc(xp_ld[t % 2], 16)
                if i == 0:
                    load_slice(S_WO + 1, cols(a["w_out"][0], SL))
            slot_free(S_RT)
            rt_w = raw[:, S_RT % 2]
            with nc.allow_non_contiguous_dma(reason="a router's few columns"):
                sp.dma_start(rt_w[:, :, 0:NG], a["router_group_w"][0].rearrange("(k p) n -> p k n", p=P)
                             ).then_inc(w_loaded, 16)
                for g in range(NG):
                    sp.dma_start(rt_w[:, :, NG + EPG * g:NG + EPG * (g + 1)],
                                 a["router_expert_w"][0, g].rearrange("(k p) n -> p k n", p=P)).then_inc(w_loaded, 16)
            load_slice(S_PG, cols(a["w_ple_gate"][0], 0))
            sp.wait_ge(tp_lo, TL_X1)
            for j in range(2):
                sp.wait_ge(x1_stored[j], 16 * (NT // 2))
            sp.dma_start(rb_bc[:, 0:NG], bcast(a["router_group_b"], NG)).then_inc(pw_ld, 16)
            sp.dma_start(rb_bc[:, NG:NLOG], bcast(a["router_expert_b"], NE)).then_inc(pw_ld, 16)
            sp.dma_start(wple, a["w_ple"][0].rearrange("(k p) n -> p k n", p=P)).then_inc(pw_ld, 16)
            sp.dma_start(pg_bc, bcast(a["ple_gate_b"], D)).then_inc(pw_ld, 16)
            def load_p(t):
                if t > 1:
                    sp.wait_ge(p_ev, t - 1)
                sp.dma_start(pnat[t % 2], a["p"][0, 0, t * P:(t + 1) * P, :]).then_inc(p_ld[t % 2], 16)
            for t in range(2):
                load_p(t)
            def expert(b):
                return sp.value_load(be_row[0:1, bass.ds(b, 1)], min_val=0, max_val=NE - 1)

            def load_weight(b, m, e, started):
                w = (a["expert_w_gate"], a["expert_w_up"], a["expert_w_down"])[m]
                if started:
                    sp.wait_ge(m_lo[(m + 1) % 3], (b + (m == 2) + -1) * WC)
                    sp.sem_inc(t_sp, 1)
                elif (b, m) == (0, 0):
                    sp.wait_ge(w_lo, WC * S_END)
                elif (b, m) == (0, 2):
                    sp.wait_ge(lg_tp, 1)
                    for j in range(2):
                        sp.wait_ge(x1_stored[j], 16 * (NT // 2))
                elif (b, m) == (1, 0):
                    for j in range(2):
                        sp.wait_ge(pp_done[j], NT)
                elif (b, m) == (1, 1):
                    for j in range(2):
                        sp.wait_ge(z2_st[j], 16 * NT)
                elif (b, m) == (1, 2):
                    sp.wait_ge(m_lo[0], WC)
                if started or b == 1:
                    sp.wait_ge(m_ld[m], b * 16)
                    sp.sem_inc(t_sp, 1)
                src = w[0, bass.ds(e, 1)].rearrange("e (p k) n -> p e (k n)", p=P)
                dst = ring.rearrange("p (r n) -> p r n", r=RING)[:, bass.ds((b * 3 + m) % RING, 1), :]
                sp.dma_start(dst, src).then_inc(m_ld[m], 16)

            def store_z2(i, t):
                sp.wait_ge(z2_ok[t % 2], i * (NT // 2) + t // 2 + 1)
                sp.dma_start(z2_d[t * P:(t + 1) * P, i * SL:(i + 1) * SL], z2p[t % 2]).then_inc(z2_st[t % 2], 16)
            for i in range(NS):
                for t in range(NT):
                    if i or t > 1:
                        store_z2(*((i, t - 2) if t > 1 else (i - 1, NT - 2 + t)))
                    sp.dma_start(x1p[t % 2], x1_d[t * P:(t + 1) * P, i * SL:(i + 1) * SL]).then_inc(xp_ld[t % 2], 16)
                    if i == 0 and t + 2 < NT:
                        load_p(t + 2)
                    if i == 1 and t == 3:
                        sp.wait_ge(nb_ok, 1)
                        e_first = expert(0)
                    if i == 1 and 3 <= t < 6:
                        load_weight(0, t - 3, e_first, False)
                if i == 0:
                    load_slice(S_PG + 1, cols(a["w_ple_gate"][0], SL))
            for t in range(NT - 2, NT):
                store_z2(NS - 1, t)

            n_blocks = sp.snap(sp.value_load(nb_i[0:1, 0:1], min_val=0, max_val=MAXB - MINB) + MINB)
            e_next = expert(1)
            for m in range(3):
                load_weight(1, m, e_next, False)
            with sp.Fori(2, n_blocks) as b:
                e_next = expert(b)
                for m in range(3):
                    load_weight(b, m, e_next, True)
            for m in range(3):
                sp.wait_ge(m_lo[m], n_blocks * WC)
                sp.sem_inc(t_sp, 1)
            for t in range(NT):
                sp.dma_start(zt[t], z2_d[t * P:(t + 1) * P, :]).then_inc(z_ld, 16)
            sp.dma_start(l2g, bcast(a["ln2_g"], D)).then_inc(l2_ld, 16)
            sp.dma_start(l2b, bcast(a["ln2_b"], D)).then_inc(l2_ld, 16)
            sp.wait_ge(y_st, n_blocks * 16 + 16)
            sp.sem_inc(t_sp, 1)

            def load_y(t):
                for c, y in enumerate((y0, y1)):
                    sp.dma_start(y[t % (NT // 2)], y_d[c * SEQ + t * P:c * SEQ + (t + 1) * P, :]
                                 ).then_inc(f_z[t % (NT // 2)], 16)
            for t in range(NT // 2):
                load_y(t)
            for t in range(NT):
                if t + NT // 2 < NT:
                    sp.wait_ge(f_var, t + 1)
                    load_y(t + NT // 2)
                sp.wait_ge(f_o[t % 2], t // 2 + 1)
                sp.dma_start(a["out"][0, t * P:(t + 1) * P, :], zo[t % 2]).then_inc(f_st[t % 2], 16)
            for j in range(2):
                sp.wait_ge(f_st[j], 16 * (NT // 2))

        @block.gpsimd
        def _(pool):
            def store(h, n, dst, src):
                pool.wait_ge(pj_free[h], n + 2)
                pool.dma_start(dst, src).then_inc(ev_stored[h], 16)

            def halves(h):
                return slice(h * SL, (h + 1) * SL)

            pool.memset(kT[:, :, 0:CHUNK], 0.0).then_inc(kt_pad, 1)
            pool.wait_ge(kt_pad, 1)
            pool.dma_start(sv_d[0:CHUNK, :].rearrange("p (h d) -> p h d", h=KVH), kT[0:CHUNK, :, 0:CHUNK]
                           ).then_inc(ot_st, 16)
            for i in range(NS):
                for c in range(CPS):
                    for h in range(2):
                        n = i * CPS + c
                        store(h, B_SQ + n, z_d[Z_SQ + n, :, halves(h)], ev[h])
            pool.wait_ge(rel_ev, 1)
            pool.dma_start(rel_d, relv[:, None, :].to_broadcast([HEADS, CHUNK, REL])).then_inc(rel_st, 16)

            def load_q(tile, j):
                pool.dma_start(qst[j], z_d[Z_SQ:Z_SQ + PAIRS, :, bass.ds(tile * P, P)].rearrange("h p n -> p h n")
                               ).then_inc(q_ld[j], 16)
            for h in range(2):
                pool.wait_ge(ev_stored[h], 16 * E_SV)
            pool.wait_ge(rel_st, 16)
            for t in range(2):
                load_q(t, t)
            for h in range(2):
                pool.wait_ge(pj_free[h], B_SV + 1)
            pool.tensor_copy(kst, kT[:, :, 0:P]).then_inc(k_st, 1)
            for t in range(NT):
                store(t % 2, B_SV + t // 2, sv_d[CHUNK + t * P:CHUNK + (t + 1) * P, :], ev[t % 2][:, 0:KVH * HD])
            for h in range(2):
                pool.wait_ge(ev_stored[h], 16 * E_GATE)
            pool.wait_ge(ot_st, 16)
            with pool.Fori(0, 4) as i:
                for j in range(4):
                    n = i * 4 + j
                    pool.wait_ge(sc_done, n + 2)
                    pool.sem_inc(t_pool, 1)
                    pool.tensor_copy(kst, kT[:, :, bass.ds((n + 1) % (2 * NT) * CHUNK, P)]).then_inc(k_st, 1)
                    if j % 2:
                        load_q((i * 2 + (j // 2 + 2)) % NT, j // 2)
                    pool.wait_ge(pv_done, n + 1)
                    pool.sem_inc(t_pool, 1)
                    pool.dma_start(vst[j % 2], sv_d[bass.ds(n * CHUNK, P), :]).then_inc(v_ld[j % 2], 16)
                    for h in range(2):
                        pool.wait_ge(pj_free[h], n + (B_GATE + 2))
                        pool.sem_inc(t_pool, 1)
                        pool.dma_start(z_d[bass.ds(n + Z_GATE, 1), :, halves(h)].rearrange("a p n -> p (a n)"),
                                       ev[h]).then_inc(ev_stored[h], 16)
                    if j % 2:
                        pool.wait_ge(ot_ev, n + 1)
                        pool.sem_inc(t_pool, 1)
                        pool.dma_start(b_d[:, :, bass.ds((i * 2 + j // 2) * P, P)].rearrange("h p n -> p h n"),
                                       oT_s).then_inc(ot_st, 16)
            pool.wait_ge(ot_st, 16 * (NT + 1))
            for j in range(2):
                pool.wait_ge(q_ld[j], 16 * (NT // 2 + 1))
            pool.wait_ge(k_st, 2 * NT + 1)
            for j in range(2):
                pool.memset(lrst[j], 1.0).then_inc(gu_one, 1)
            with pool.Fori(0, 3) as i:
                for t in range(NT):
                    pool.wait_ge(pj_free[t % 2], i * (NT // 2) + (B_KV + t // 2 + 2))
                    pool.sem_inc(t_pool, 1)
                    pool.dma_start(kv_d[t * P:(t + 1) * P, bass.ds(i * SL, SL)], ev[t % 2]
                                   ).then_inc(ev_stored[t % 2], 16)
            for h in range(2):
                store(h, B_LR, lr_d[:, halves(h)], ev[h][0:RANK, :])
            for c in range(CPS):
                for h in range(2):
                    store(h, B_GQ + c, z_d[Z_GQ + c, :, halves(h)], ev[h])

            for i in range(NS):
                for t in range(NT):
                    pool.wait_ge(a_ok[t % 2], i * (NT // 2) + t // 2 + 1)
                    pool.dma_start(a_d[t * P:(t + 1) * P, i * SL:(i + 1) * SL], apc[t % 2]).then_inc(a_st[t % 2], 16)
            for t in range(NT):
                pool.wait_ge(x1_ready[t % 2], t // 2 + 1)
                pool.dma_start(x1_d[t * P:(t + 1) * P, :], nat[t % 2]).then_inc(x1_stored[t % 2], 16)

            def name_slots(c, t):
                pool.indirect_dma_start(
                    out=slot_d, out_offset=bass.IndirectOffsetOnAxis(ap=slot_i[:, c, t:t + 1], axis=0),
                    in_=toki[:, c, t, :], in_offset=None).then_inc(scat, 16)

            def gather(b, k):
                pool.tensor_copy(idx, slots[:, bass.ds(b, 1), 0]).then_inc(idx_ok, 1)
                pool.wait_ge(idx_ok, k + 1)
                pool.sem_inc(t_pool, 1)
                pool.indirect_dma_start(out=xb, out_offset=None, in_=x1_d,
                                        in_offset=bass.IndirectOffsetOnAxis(ap=idx, axis=0)).then_inc(xb_ld, 16)

            pool.wait_ge(zs_st, 16)
            pool.wait_ge(c_ld, CONSTS)
            pool.wait_ge(slots_ok, 2)
            for c in range(2):
                for t in range(NT):
                    name_slots(c, t)
            pool.wait_ge(scat, 16 * 2 * NT)
            with nc.allow_non_contiguous_dma(reason="two numbers of each slot"):
                pool.dma_start(slots, slot_d.rearrange("(b p) c -> p b c", p=P)).then_inc(y_st, 16)
            for j in range(2):
                pool.wait_ge(x1_stored[j], 16 * (NT // 2))
            pool.wait_ge(nb_ok, 1)
            pool.wait_ge(y_st, 16)
            gather(0, 0)
            n_blocks = pool.snap(pool.value_load(nb_i[0:1, 0:1], min_val=0, max_val=MAXB - MINB) + MINB)

            def scatter(b, k):
                pool.wait_ge(y_st, b * 16 + 16)
                pool.sem_inc(t_pool, 1)
                pool.tensor_copy(idy, slots[:, bass.ds(b, 1), 1]).then_inc(idx_ok, 1)
                pool.wait_ge(idx_ok, k + 1)
                pool.sem_inc(t_pool, 1)
                pool.wait_ge(y_ev, b * 2 + 4)
                pool.sem_inc(t_pool, 1)
                pool.indirect_dma_start(out=y_d, out_offset=bass.IndirectOffsetOnAxis(ap=idy, axis=0),
                                        in_=y_s, in_offset=None).then_inc(y_st, 16)
            for b in range(1, 3):
                pool.wait_ge(xt_done, 2 * b)
                gather(b, b)
            with pool.Fori(3, n_blocks) as b:
                pool.wait_ge(xt_done, b * 2)
                pool.sem_inc(t_pool, 1)
                gather(b, b * 2 + -3)
                scatter(b + -3, b * 2 + -2)
            for k in range(3):
                scatter(pool.snap(n_blocks + (k - 3)), n_blocks * 2 + (k - 3))

            pool.wait_ge(l2_ld, 32)
            for t in range(NT):
                j = t % 2
                pool.wait_ge(f_n, t + 1)
                pool.tensor_tensor(zn[j], zn[j], l2g, ALU.mult).then_inc(f_g, 1)
                pool.wait_ge(f_g, t + 1)
                if t > 1:
                    pool.wait_ge(f_st[j], 16 * (t // 2))
                pool.tensor_tensor(zo[j], zn[j], l2b, ALU.add).then_inc(f_o[j], 1)

        acts = (act_h, act_l)
        wgts = (wgt_h, wgt_l)
        THREE = ((0, 0), (0, 1), (1, 0))

        @block.tensor
        def _(pe):
            def one_pass(s, out, b, n, left, right, first, last, ready=None):
                pe.wait_ge(pj_free[b], n + 1)
                pe.sem_inc(t_pe, 1)
                for k in range(KC):
                    if ready is not None:
                        pe.wait_ge(tp_lo, ready + k + 1)
                    if first and k % 2 == 0:
                        pe.wait_ge(w_lo, s * WC + (k // 2 + 1))
                        pe.sem_inc(t_pe, 1)
                    for x, y in THREE:
                        ins = pe.matmul(out, left(x, k), right(y, k), start=k == 0 and (x, y) == (0, 0),
                                        stop=k == KC - 1 and x == 1)
                    if last and k % 2 and k < KC - 1:
                        ins.then_inc(w_used, 1)
                ins.then_inc(pj_done[b], 1)

            def to_channels(s, c, h, n, first=False, last=False, ready=None):
                one_pass(s, bank(h), h, n,
                         lambda x, k: wgts[x][:, k, c * P:(c + 1) * P],
                         lambda x, k: acts[x][:, k, h * SL:(h + 1) * SL], first, last, ready)

            def to_tokens(s, t, n, first=False, last=False, ready=None, c0=0, w=SL):
                one_pass(s, bank(t % 2)[:, 0:w], t % 2, n,
                         lambda x, k: acts[x][:, k, t * P:(t + 1) * P],
                         lambda x, k: wgts[x][:, k, c0:c0 + w], first, last, ready)

            def slice_channels(s, n, ready=None):
                for c in range(CPS):
                    for h in range(2):
                        to_channels(s, c, h, n + c, (c, h) == (0, 0), (c, h) == (CPS - 1, 1),
                                    ready if (c, h) == (0, 0) else None)

            def slice_tokens(s, n, ready=None, after=None):
                for t in range(NT):
                    to_tokens(s, t, n + t // 2, t == 0, t == NT - 1,
                              ready + (t > 0) * KC if ready is not None and t % (NT // 2) == 0 else None)
                    if after:
                        after(t)

            def transposes(src, t, low):
                for h in range(2):
                    pe.wait_ge(tp_lo, low + h)
                    for k in range(KC // 2):
                        ins = pe.transpose(bank(2 + 2 * (t % 2) + h)[:, k * P:(k + 1) * P],
                                           src[:, (h * 4 + k) * P:(h * 4 + k + 1) * P], ident)
                    ins.then_inc(tp_done, 1)

            pe.sem_inc(tp_done, 4)
            pe.sem_inc(tp_lo, 4)
            for b in range(2):
                pe.sem_inc(pj_free[b], 1)
            pe.sem_inc(sc_done, 1)
            pe.sem_inc(pv_done, 2)

            pe.wait_ge(cst_ld, 16)
            for t in range(NT):
                pe.wait_ge(x_ld[t], 16)
                transposes(x_nat[t], t, 2 * t + 1)

            pe.wait_ge(tp_lo, TL_X)
            with pe.Fori(0, NS) as i:
                slice_channels(i + S_SQ, i * CPS + B_SQ)
            pe.wait_ge(c_ld, CONSTS)
            pe.matmul(ps[0:HEADS, 7, 0:REL], relt, buck, start=True, stop=True).then_inc(rel_mm, 1)

            for c in range(KVH // 2):
                for h in range(2):
                    to_channels(S_SKV, c, h, B_SK + c, (c, h) == (0, 0))
            for t in range(NT):
                to_tokens(S_SKV, t, B_SV + t // 2, False, t == NT - 1, c0=KVH * HD, w=KVH * HD)

            def scores(n, half, tile_par, tiles):
                pe.wait_ge(q_ld[tile_par], tiles * 16)
                pe.sem_inc(t_pe, 1)
                pe.wait_ge(k_st, n + 1)
                pe.sem_inc(t_pe, 1)
                q = qst[tile_par]
                for h4 in range(2):
                    for p4 in range(4):
                        for r in range(2):
                            p = ((h4 + r) % 2) * 4 + p4
                            lo = CHUNK * r
                            ins = pe.matmul(bank(4 + p // 4)[lo:lo + CHUNK, (p % 4) * P:(p % 4 + 1) * P],
                                            q[lo:lo + CHUNK, p, half * CHUNK:(half + 1) * CHUNK],
                                            kst[lo:lo + CHUNK, p // 2, :], start=True, stop=True)
                ins.then_inc(sc_done, 1)

            scores(0, 0, 0, 1)
            with pe.Fori(0, 4) as i:
                for j in range(4):
                    n = i * 4 + j
                    for h in range(2):
                        to_channels(i + S_GATE, j, h, n + B_GATE, (j, h) == (0, 0), (j, h) == (3, 1))
                    pe.wait_ge(p_ok, n + 1)
                    pe.sem_inc(t_pe, 1)
                    for p in range(PAIRS):
                        ins = pe.transpose(bank(2 + p // 4)[:, (p % 4) * P:(p % 4 + 1) * P],
                                           pr_s[:, p * P:(p + 1) * P], ident)
                    ins.then_inc(pt_done, 1)
                    scores(n + 1, (j + 1) % 2, (j + 1) // 2 % 2, i + (1 + (j + 1) // 4))
                    pe.wait_ge(v_ld[j % 2], i * 32 + 16 * (j // 2 + 1))
                    pe.sem_inc(t_pe, 1)
                    pe.wait_ge(pt_ev, n + 1)
                    pe.sem_inc(t_pe, 1)
                    pT3 = pT_s.rearrange("p (h n) -> p h n", h=PAIRS)
                    for r in range(2):
                        for g in range(KVH):
                            ins = pe.matmul(bank(6)[CHUNK * r:CHUNK * (r + 1), g * P:(g + 1) * P],
                                            vst[j % 2][:, g * HD:(g + 1) * HD],
                                            pT3[:, 2 * g:2 * g + 2, CHUNK * r:CHUNK * (r + 1)],
                                            start=True, stop=True)
                    ins.then_inc(pv_done, 1)

            with pe.Fori(0, 3) as i:
                slice_tokens(i + S_KV, i * (NT // 2) + B_KV)
            for h in range(2):
                to_channels(S_LR, 0, h, B_LR, h == 0, h == 1)
            slice_channels(S_GQ, B_GQ)

            for b in range(2):
                pe.wait_ge(pj_free[b], B_R + 1)
            pe.wait_ge(gu_ld, 32)

            def gate_logits(t, j, tiles):
                pe.wait_ge(g_ld[j], tiles * 32)
                pe.sem_inc(t_pe, 1)
                if not (isinstance(t, int) and t == 0):
                    pe.wait_ge(gg_dec, t)
                    pe.sem_inc(t_pe, 1)
                pe.matmul(bank(0), lrst[j][0:RANK + 1, :], gup[0:RANK + 1, :], start=True, stop=True
                          ).then_inc(gg_mm, 1)

            def decay_sums(t):
                pe.wait_ge(gg_la, t + 1)
                pe.sem_inc(t_pe, 1)
                for h in range(GH):
                    pe.matmul(bank(0)[:, 2 * h:2 * h + 2], gla_l[:, h * GK:(h + 1) * GK],
                              cst[:, K_CH:K_CH + 2], start=True, stop=True)
                pe.matmul(bank(1), cst[:, K_SUF:K_SUF + P], gla_l, start=True, stop=True).then_inc(gg_suf, 1)

            def updates(t, j):
                pe.wait_ge(gg_kd, t + 1)
                pe.sem_inc(t_pe, 1)
                for c in range(2):
                    lo = CHUNK * c
                    for h in range(GH):
                        ins = pe.matmul(bank(2 + 2 * c, 2)[:, h * GV:(h + 1) * GV],
                                        kdec[lo:lo + CHUNK, h * GK:(h + 1) * GK],
                                        kvst[j][lo:lo + CHUNK, SL + h * GV:SL + (h + 1) * GV],
                                        start=True, stop=True)
                    ins.then_inc(gu_mm, 1)

            def outputs(t, j, tiles):
                pe.wait_ge(gq_ld[j], tiles * 16)
                pe.sem_inc(t_pe, 1)
                pe.wait_ge(go_ev, t + 1)
                pe.sem_inc(t_pe, 1)
                for c, st in enumerate((st_a, st_b)):
                    pe.wait_ge(gs_up, t * 8 + 4 * (c + 1))
                    pe.sem_inc(t_pe, 1)
                    for h in range(GH):
                        ins = pe.matmul(bank(6, 2)[CHUNK * c:CHUNK * (c + 1), h * GV:(h + 1) * GV],
                                        gqst[j][:, h, CHUNK * c:CHUNK * (c + 1)], st[:, h, :],
                                        start=True, stop=True)
                ins.then_inc(go_mm, 1)
            gate_logits(0, 0, 1)
            decay_sums(0)
            with pe.Fori(0, NT // 2 - 1) as v:
                for j in range(2):
                    t = v * 2 + j
                    gate_logits(t + 1, 1 - j, v + (1 + j))
                    updates(t, j)
                    decay_sums(t + 1)
                    outputs(t, j, v + 1)
            gate_logits(NT - 1, 1, NT // 2)
            updates(NT - 2, 0)
            decay_sums(NT - 1)
            outputs(NT - 2, 0, NT // 2)
            updates(NT - 1, 1)
            outputs(NT - 1, 1, NT // 2)

            slice_tokens(S_R, B_R)

            def transpose_a(t):
                pe.wait_ge(n_loaded[t % 2], 16 * (t // 2 + 2))
                transposes(nat[t % 2], t, TL_X + 2 * t - 3)
            slice_tokens(S_R + 1, B_R + NT // 2, after=lambda t: transpose_a(t - 4) if t > 3 else None)
            for t in range(NT - 4, NT):
                transpose_a(t)
            pe.wait_ge(tp_lo, TL_A)
            with pe.Fori(0, NS) as i:
                slice_channels(i + S_WG, i * CPS + B_WG)
            for i in range(NS):
                slice_channels(S_WS + i, B_WS + i * CPS, TL_A if i == 0 else None)
            slice_tokens(S_WO, B_WO, TL_B)

            def transpose_x1(t):
                pe.wait_ge(x1_ready[t % 2], t // 2 + 1)
                transposes(nat[t % 2], t, TL_M + 2 * t - 3)
            slice_tokens(S_WO + 1, B_WO + NT // 2, after=lambda t: transpose_x1(t - 2) if t > 1 else None)
            transpose_x1(NT - 2)
            to_channels(S_RT, 0, 0, B_RT, True, False)
            transpose_x1(NT - 1)
            pe.wait_ge(tp_lo, TL_X1)
            to_channels(S_RT, 0, 1, B_RT, False, True)
            for b in range(2):
                pe.wait_ge(pj_free[b], B_PG + 1)
            for t in range(NT):
                ins = pe.transpose(bank(2 + t // 4)[:, (t % 4) * P:(t % 4 + 1) * P], lgT[:, t * P:(t + 1) * P], ident)
            ins.then_inc(lg_tp, 1)

            def transpose_p(t):
                pe.wait_ge(p_ld[t % 2], 16 * (t // 2 + 1))
                if t > 1:
                    pe.wait_ge(p_ev, t - 1)
                for k in range(PKC):
                    ins = pe.transpose(bank(2 + t % 2)[:, k * P:(k + 1) * P], pnat[t % 2][:, k * P:(k + 1) * P], ident)
                ins.then_inc(p_tp, 1)
            for b in range(2):
                pe.sem_inc(pp_free[b], 1)
            for i in range(NS):
                for t in range(NT):
                    n = i * (NT // 2) + t // 2
                    to_tokens(S_PG + i, t, B_PG + n, t == 0, t == NT - 1)
                    if (i, t) == (0, 0):
                        pe.wait_ge(pw_ld, 64)
                        pe.wait_ge(r_mx, 1)
                        transpose_p(0)
                        transpose_p(1)
                    if i == 0:
                        pe.wait_ge(p_ev, t + 1)
                    pe.wait_ge(pp_free[t % 2], n + 1)
                    for k in range(PKC):
                        ins = pe.matmul(bank(4 + t % 2), pT[:, k, t * P:(t + 1) * P],
                                        wple[:, k, i * SL:(i + 1) * SL], start=k == 0, stop=k == PKC - 1)
                    ins.then_inc(pp_done[t % 2], 1)
                    if i == 0 and t + 2 < NT:
                        transpose_p(t + 2)
                    if (i, t) == (0, 2):
                        pe.wait_ge(r_oh, 1)
                        o2 = ohs.rearrange("p t e -> p (t e)")
                        pe.matmul(bank(6)[:, 0:NT * NE], cst[:, K_ERL:K_ERL + P], o2, start=True, stop=True)
                        pe.matmul(bank(7)[:, 0:NT * NE], cst[:, K_ONE:K_ONE + P], o2, start=True, stop=True
                                  ).then_inc(r_mm, 1)

            blk = (blk_h, blk_l)
            xb3 = xb.rearrange("p (n k) -> p k n", k=KC)
            hid3 = hid.rearrange("p (n k) -> p k n", k=FC)
            uw, dw = (u_h, u_l), (d_h, d_l)

            def x_transposes(b):
                pe.wait_ge(xb_ld, b * 16 + 16)
                pe.sem_inc(t_pe, 1)
                for h in range(2):
                    for k in range(KC // 2):
                        ins = pe.transpose(bank(2 + h)[:, k * P:(k + 1) * P], xb3[:, h * 4 + k, :], ident)
                    ins.then_inc(xt_done, 1)

            def up_proj(b, m, w, done):
                for k in range(KC):
                    if k % 2 == 0:
                        pe.wait_ge(m_lo[m], b * WC + (k // 2 + 1))
                        pe.sem_inc(t_pe, 1)
                    for x, y in THREE:
                        ins = pe.matmul(bank(m), blk[x][:, k, :], w[y][:, k, :],
                                        start=k == 0 and (x, y) == (0, 0), stop=k == KC - 1 and x == 1)
                    if k % 2 and k < KC - 1:
                        ins.then_inc(m_used[m], 1)
                ins.then_inc(done, 1)

            def down_proj(b):
                pe.wait_ge(ht_lo, b + 1)
                pe.sem_inc(t_pe, 1)
                pe.wait_ge(y_ev, b * 2 + 2)
                pe.sem_inc(t_pe, 1)
                for k in range(FC):
                    pe.wait_ge(m_lo[2], b * WC + (k + 1))
                    pe.sem_inc(t_pe, 1)
                    for h in range(2):
                        for x, y in THREE:
                            ins = pe.matmul(bank(5 + h), blk[x][:, KC + k, :], dw[y][:, k, h * SL:(h + 1) * SL],
                                            start=k == 0 and (x, y) == (0, 0), stop=k == FC - 1 and x == 1)
                    if k < FC - 1:
                        ins.then_inc(m_used[2], 1)
                ins.then_inc(y_done, 1)

            def step(b, first, last):
                pe.wait_ge(xt_lo, b * 2 + 2)
                pe.sem_inc(t_pe, 1)
                if not first:
                    pe.wait_ge(sl_ok, b)
                    pe.sem_inc(t_pe, 1)
                up_proj(b, 0, wgts, gm_done)
                if not first:
                    pe.wait_ge(h_ok, b)
                    pe.sem_inc(t_pe, 1)
                up_proj(b, 1, uw, um_done)
                if not last:
                    x_transposes(b + 1)
                if not first:
                    down_proj(b - 1)
                pe.wait_ge(h_ok, b + 1)
                pe.sem_inc(t_pe, 1)
                for k in range(FC):
                    ins = pe.transpose(bank(4)[:, k * P:(k + 1) * P], hid3[:, k, :], ident)
                ins.then_inc(ht_done, 1)

            pe.sem_inc(y_ev, 2)
            pe.wait_ge(nb_ok, 1)
            last_b = pe.snap(pe.value_load(nb_i[0:1, 0:1], min_val=0, max_val=MAXB - MINB) + (MINB - 1))
            x_transposes(0)
            step(0, True, False)
            with pe.Fori(1, last_b) as b:
                step(b, False, False)
            step(last_b, False, True)
            down_proj(last_b)

        @block.scalar
        def _(act):
            own = Steps()

            def func(out, in_, f=ACT.Copy, **kw):
                return act.activation(out, in_, f, **kw)

            def split(s, n_last, w=SL):
                act.wait_ge(w_loaded, loaded(s))
                act.sem_inc(t_act, 1)
                for c in range(WC):
                    if c == WC - 1:
                        if n_last is not None:
                            act.wait_ge(pj_done[1], n_last + 1)
                            act.sem_inc(t_act, 1)
                    elif n_last is not None:
                        act.wait_ge(w_used, s * (WC - 1) + (c - 1) - (WC - 3))
                        act.sem_inc(t_act, 1)
                    src = raw[:, s % 2, 2 * c:2 * c + 2, 0:w] if isinstance(s, int) else (
                        raw[:, bass.ds(s % 2, 1), 2 * c:2 * c + 2, 0:w].rearrange("p a k n -> p (a k) n"))
                    func(wgt_h[:, 2 * c:2 * c + 2, 0:w], src).then_inc(w_hi, 1)

            def tile_high(t, h, q):
                act.wait_ge(tp_done, q)
                func(act_h[:, 4 * h:4 * h + 4, t * P:(t + 1) * P],
                     bank(2 + 2 * (t % 2) + h).rearrange("p (k n) -> p k n", k=4)).then_inc(tp_hi, 1)

            def evac(h, n, m, f=ACT.Copy, w=SL, **kw):
                act.wait_ge(pj_done[h], n + 1)
                act.sem_inc(t_act, 1)
                if not (isinstance(m, int) and m == 0):
                    act.wait_ge(ev_stored[h], m * 16)
                    act.sem_inc(t_act, 1)
                func(ev[h][:, 0:w], bank(h)[:, 0:w], f, **kw).then_inc(pj_free[h], 1)

            for t in range(NT):
                for h in range(2):
                    tile_high(t, h, 2 * t + h + 5)
            split(0, None)
            for i in range(NS):
                for c in range(CPS):
                    for h in range(2):
                        if (c, h) == (CPS - 1, 1):
                            split(i + 1, B_SQ + i * CPS + c)
                        n = i * CPS + c
                        evac(h, B_SQ + n, E_SQ + n, scale=HD ** -0.5)
            act.wait_ge(rel_mm, 1)
            func(relv, ps[0:HEADS, 7, 0:REL]).then_inc(rel_ev, 1)
            act.wait_ge(kt_pad, 1)
            for c in range(KVH // 2):
                for h in range(2):
                    act.wait_ge(pj_done[h], B_SK + c + 1)
                    for g in range(2):
                        for r in range(2):
                            ins = func(kT[r * HD:(r + 1) * HD, 2 * c + g, CHUNK + h * SL:CHUNK + (h + 1) * SL],
                                       bank(h)[g * HD:(g + 1) * HD, :])
                    ins.then_inc(pj_free[h], 1)
            for t in range(NT):
                if t == NT - 1:
                    split(S_GATE, B_SV + t // 2)
                evac(t % 2, B_SV + t // 2, E_SV + t // 2, w=KVH * HD)

            act.wait_ge(c_ld, CONSTS)
            with act.Fori(0, 4) as i:
                for j in range(4):
                    n = i * 4 + j
                    act.wait_ge(mx_ok, n + 1)
                    act.sem_inc(t_act, 1)
                    func(pr_s, sc_s, ACT.Exp)
                    func(s_es, s_sd, ACT.Exp).then_inc(e_ok, 1)
                    for h in range(2):
                        if (j, h) == (3, 1):
                            split(i + (S_GATE + 1), n + B_GATE)
                        evac(h, n + B_GATE, n + E_GATE, ACT.Identity,
                             bias=gbias[:, bass.ds(n, 1)])
                    act.wait_ge(pt_done, n + 1)
                    act.sem_inc(t_act, 1)
                    func(pT_s, bank(2, 2)).then_inc(pt_ev, 1)
            def evac_kv(i, width):
                for t in range(NT):
                    n = i * (NT // 2) + t // 2
                    if t == NT - 1:
                        split(i + (S_KV + 1), n + B_KV, width)
                    evac(t % 2, n + B_KV, n + E_KV)
            with act.Fori(0, 2) as i:
                evac_kv(i, SL)
            evac_kv(2, P)
            evac(0, B_LR, E_LR)
            split(S_GQ, B_LR)
            evac(1, B_LR, E_LR)
            for c in range(CPS):
                for h in range(2):
                    if (c, h) == (CPS - 1, 1):
                        split(S_R, B_GQ + c)
                    evac(h, B_GQ + c, E_GQ + c, scale=GK ** -0.5)

            def decays(t, j, looped):
                g = gla_t[j]
                act.wait_ge(gg_mm, t + 1)
                act.sem_inc(t_act, 1)
                for x, fn, kw in ((bank(0), ACT.Abs, {}), (g, ACT.Exp, {"scale": -1.0})):
                    func(g, x, fn, **kw).then_inc(act_own, 1)
                    act.wait_ge(act_own, own.done())
                    if looped:
                        act.sem_inc(t_act, 1)
                func(g, g, ACT.Ln, bias=1.0).then_inc(gg_abs, 1)
                act.wait_ge(gg_suf, t + 1)
                act.sem_inc(t_act, 1)
                func(g, bank(1), ACT.Exp, scale=1.0 / TAU)
                func(gam[j].rearrange("p h c -> p (h c)"), bank(0)[:, 0:2 * GH], ACT.Exp, scale=1.0 / TAU
                     ).then_inc(gg_dec, 1)

            def squares(t):
                act.wait_ge(go_mm, t + 1)
                act.sem_inc(t_act, 1)
                func(o_q, bank(6, 2), ACT.Square).then_inc(go_sq, 1)
            decays(0, 0, False)
            with own.loop(act, NT // 2 - 1, 4) as v:
                for j in range(2):
                    decays(v * 2 + (j + 1), 1 - j, True)
                    squares(v * 2 + j)
            decays(NT - 1, 1, False)
            squares(NT - 2)
            squares(NT - 1)
            act.wait_ge(rs_v, 1)
            func(ssq, ssq, ACT.Sqrt).then_inc(rs_s, 1)
            for i in range(NS):
                for t in range(NT):
                    n = i * (NT // 2) + t // 2
                    if t == NT - 1:
                        split(S_R + 1 + i, B_R + n)
                    act.wait_ge(pj_done[t % 2], B_R + n + 1)
                    if n:
                        act.wait_ge(a_ok[t % 2], n)
                    func(rsil[t % 2], bank(t % 2), ACT.Silu).then_inc(pj_free[t % 2], 1)
                    if i == NS - 1 and t > 3:
                        for h in range(2):
                            tile_high(t - 4, h, 2 * NT + 2 * (t - 4) + h + 5)
            for t in range(NT - 4, NT):
                for h in range(2):
                    tile_high(t, h, 2 * NT + 2 * t + h + 5)

            def sigmoids(base, nb, s):
                for i in range(NS):
                    for c in range(CPS):
                        for h in range(2):
                            k = base + i * CPS + c
                            act.wait_ge(gt_ld[h], 16 * (k + 1))
                            act.wait_ge(pj_free[h], nb + i * CPS + c + 1)
                            func(gsg[h], gld[h], ACT.Sigmoid).then_inc(gt_free[h], 1)
                            if (c, h) == (CPS - 1, 0):
                                split(s + 1 + i, nb + i * CPS + c)
            sigmoids(0, B_WG, S_WG)
            for c in range(KC):
                act.wait_ge(b_ld[c % 4], 16 * (c // 4 + 2))
                func(act_h[:, c, :], bst[c % 4]).then_inc(tp_hi, 1)
            sigmoids(KC, B_WS, S_WS)
            for h in range(2):
                act.wait_ge(pj_done[h], B_WS + KC)
            for h in range(2):
                for c in range(KC):
                    act.wait_ge(m_ok, 2 * c + h + 1)
                    func(act_h[:, c, h * SL:(h + 1) * SL], mT[:, c, h * SL:(h + 1) * SL]).then_inc(tp_hi, 1)
            split(S_WO + 1, B_WO + 3)
            for t in range(NT + 2):
                if t == NT - 1:
                    split(S_RT, B_WO + NT - 1, NLOG)
                if t < NT:
                    act.wait_ge(ln_v, t + 1)
                    func(rstd[:, t:t + 1], rstd[:, t:t + 1], ACT.Sqrt).then_inc(ln_s, 1)
                    act.wait_ge(ln_r, t + 1)
                    if t > 1:
                        act.wait_ge(x1_ready[t % 2], t // 2)
                    func(xn[t % 2], y_n[:, t, :], ACT.Identity, bias=nmr[:, t:t + 1], scale=rstd[:, t:t + 1]
                         ).then_inc(xn_ok, 1)
                if t > 1:
                    for h in range(2):
                        tile_high(t - 2, h, 4 * NT + 2 * (t - 2) + h + 5)
            for h in range(2):
                act.wait_ge(pj_done[h], B_RT + 1)
                func(lgT[:, h * SL:(h + 1) * SL], bank(h)).then_inc(pj_free[h], 1)
            split(S_PG, B_RT)
            act.wait_ge(r_mx, 1)
            func(g_e, g_e, ACT.Exp).then_inc(r_ex, 1)
            act.wait_ge(r_dif, 1)
            func(e_mx[1], e_mx[1], ACT.Exp).then_inc(r_e2, 1)

            def evac_p(t):
                act.wait_ge(p_tp, t + 1)
                func(pT[:, :, t * P:(t + 1) * P], bank(2 + t % 2)[:, 0:PLE].rearrange("p (k n) -> p k n", k=PKC)
                     ).then_inc(p_ev, 1)
            for t in range(2):
                evac_p(t)
            for i in range(NS):
                for t in range(NT):
                    n = i * (NT // 2) + t // 2
                    act.wait_ge(pj_free[t % 2], B_PG + n + 2)
                    func(gpre[t % 2], gpre[t % 2], ACT.Sigmoid).then_inc(gs_ok[t % 2], 1)
                    if i == 0 and t + 2 < NT:
                        evac_p(t + 2)
                    if i == 0 and t == NT - 2:
                        split(S_PG + 1, B_PG + NT // 2 - 1)

            act.wait_ge(nb_ok, 1)
            last_b = act.snap(act.value_load(nb_i[0:1, 0:1], min_val=0, max_val=MAXB - MINB) + (MINB - 1))

            def split_expert(m, b, dst, src, done, free):
                act.wait_ge(m_ld[m], b * 16 + 16)
                act.sem_inc(t_act, 1)
                w = dst.shape[1] // WC
                for c in range(WC):
                    if free:
                        if c < WC - 1:
                            act.wait_ge(m_used[m], b * (WC - 1) + (c + 2 - WC))
                            act.sem_inc(t_act, 1)
                        else:
                            act.wait_ge(done, b)
                            act.sem_inc(t_act, 1)
                    func(dst[:, w * c:w * (c + 1), :], arrived(src, m, b, slice(w * c, w * (c + 1)))).then_inc(m_hi[m], 1)

            def x_high(b, free):
                if free:
                    act.wait_ge(um_done, b)
                    act.sem_inc(t_act, 1)
                for h in range(2):
                    act.wait_ge(xt_done, b * 2 + (h + 1))
                    act.sem_inc(t_act, 1)
                    func(blk_h[:, 4 * h:4 * h + 4, :], bank(2 + h).rearrange("p (k n) -> p k n", k=4)
                         ).then_inc(xt_hi, 1)

            def y_out(b):
                act.wait_ge(y_done, b + 1)
                act.sem_inc(t_act, 1)
                act.wait_ge(y_st, b * 16 + 16)
                act.sem_inc(t_act, 1)
                for h in range(2):
                    func(y_s[:, h * SL:(h + 1) * SL], bank(5 + h)).then_inc(y_ev, 1)

            def step(b, first, last):
                if not last and not first:
                    split_expert(0, b + 1, wgt_h, ring_up, gm_done, True)
                act.wait_ge(gm_done, b + 1)
                act.sem_inc(t_act, 1)
                if first:
                    for j in range(2):
                        act.wait_ge(z2_st[j], 16 * NT)
                else:
                    act.wait_ge(h_ok, b)
                    act.sem_inc(t_act, 1)
                func(sig, bank(0), ACT.Silu).then_inc(sl_ok, 1)
                if first:
                    split_expert(2, 0, d_h, ring_down, y_done, False)
                    split_expert(0, 1, wgt_h, ring_up, gm_done, True)
                if not last:
                    split_expert(1, b + 1, u_h, ring_up, um_done, True)
                    x_high(b + 1, True)
                if not first:
                    split_expert(2, b, d_h, ring_down, y_done, True)
                    y_out(b - 1)
                act.wait_ge(ht_done, b + 1)
                act.sem_inc(t_act, 1)
                func(blk_h[:, KC:KC + FC, :], bank(4).rearrange("p (k n) -> p k n", k=FC)).then_inc(ht_hi, 1)

            act.wait_ge(m_ld[0], 16)
            for c in range(WC):
                if c < WC - 1:
                    act.wait_ge(w_used, (S_END - 1) * (WC - 1) + c + 1)
                else:
                    act.wait_ge(pj_done[1], B_PG + NT)
                func(wgt_h[:, 2 * c:2 * c + 2, :], arrived(ring_up, 0, 0, slice(2 * c, 2 * c + 2))).then_inc(m_hi[0], 1)
            x_high(0, False)
            split_expert(1, 0, u_h, ring_up, um_done, False)
            step(0, True, False)
            with act.Fori(1, last_b) as b:
                step(b, False, False)
            step(last_b, False, True)
            y_out(last_b)

            for t in range(NT):
                j = t % 2
                act.wait_ge(f_var, t + 1)
                func(frs[:, j, :], frs[:, j, :], ACT.Sqrt).then_inc(f_sq, 1)
                if t > 1:
                    act.wait_ge(f_g, t - 1)
                    act.wait_ge(f_o[j], t // 2)
                act.wait_ge(f_rs, t + 1)
                func(zn[j], zt[t], ACT.Identity, bias=fnm[:, j, :], scale=frs[:, j, :]).then_inc(f_n, 1)

        @block.vector
        def _(dve):
            own = Steps()

            def over(v, n):
                return v[:, :, None].to_broadcast([v.shape[0], v.shape[1], n])

            def along(v, n):
                return v[:, None, :].to_broadcast([v.shape[0], n, v.shape[1]])

            def heads_of(v, n):
                return v.rearrange("p (a n) -> p a n", n=n)

            def low(s, w=SL):
                for c in range(WC):
                    dve.wait_ge(w_hi, s * WC + (c + 1))
                    dve.sem_inc(t_dve, 1)
                    src = raw[:, s % 2, 2 * c:2 * c + 2, 0:w] if isinstance(s, int) else (
                        raw[:, bass.ds(s % 2, 1), 2 * c:2 * c + 2, 0:w].rearrange("p a k n -> p (a k) n"))
                    dve.tensor_tensor(wgt_l[:, 2 * c:2 * c + 2, 0:w], src, f(wgt_h[:, 2 * c:2 * c + 2, 0:w]),
                                    ALU.subtract).then_inc(w_lo, 1)

            def tile_low(t, h, q):
                dve.wait_ge(tp_hi, q)
                dve.tensor_tensor(act_l[:, 4 * h:4 * h + 4, t * P:(t + 1) * P],
                                  bank(2 + 2 * (t % 2) + h).rearrange("p (k n) -> p k n", k=4),
                                  f(act_h[:, 4 * h:4 * h + 4, t * P:(t + 1) * P]), ALU.subtract).then_inc(tp_lo, 1)

            for t in range(NT):
                for h in range(2):
                    tile_low(t, h, 2 * t + h + 1)
            low(0)
            low(1)
            low(S_SKV)
            dve.wait_ge(bias_ld, 32)
            dve.tensor_copy(bias[:, 0, :], bias[:, 1, :]).then_inc(dve_own, 1)
            dve.wait_ge(dve_own, own.done())
            dve.memset(heads_of(bias[:, 0, :], P)[:, :, 0:CHUNK], NEG).then_inc(dve_own, 1)
            dve.wait_ge(dve_own, own.done())
            low(S_GATE)

            dve.wait_ge(c_ld, CONSTS)
            with own.loop(dve, 4, 28) as i:
                for j in range(4):
                    n = i * 4 + j
                    dve.wait_ge(sc_done, n + 2)
                    dve.sem_inc(t_dve, 1)
                    b = bias[:, bass.ds((i + 3) // 4, 1), :].rearrange("p a n -> p (a n)") if j == 0 else bias[:, 1, :]
                    dve.tensor_tensor(sc_s, bank(4, 2), b, ALU.add).then_inc(dve_own, 1)
                    dve.wait_ge(dve_own, own.done())
                    dve.sem_inc(t_dve, 1)
                    dve.tensor_reduce(s_mx, heads_of(sc_s, P), AX.X, ALU.max).then_inc(dve_own, 1)
                    dve.wait_ge(dve_own, own.done())
                    dve.sem_inc(t_dve, 1)
                    dve.tensor_tensor(s_mx, s_mx, sink, ALU.max).then_inc(dve_own, 1)
                    dve.wait_ge(dve_own, own.done())
                    dve.sem_inc(t_dve, 1)
                    dve.tensor_tensor(s_sd, sink, s_mx, ALU.subtract).then_inc(dve_own, 1)
                    dve.wait_ge(dve_own, own.done())
                    dve.sem_inc(t_dve, 1)
                    dve.tensor_tensor(heads_of(sc_s, P), heads_of(sc_s, P), over(s_mx, P), ALU.subtract).then_inc(mx_ok, 1)
                    dve.wait_ge(e_ok, n + 1)
                    dve.sem_inc(t_dve, 1)
                    dve.tensor_reduce(s_den, heads_of(pr_s, P), AX.X, ALU.add).then_inc(dve_own, 1)
                    dve.wait_ge(dve_own, own.done())
                    dve.sem_inc(t_dve, 1)
                    dve.tensor_tensor(s_den, s_den, s_es, ALU.add).then_inc(dve_own, 1)
                    dve.wait_ge(dve_own, own.done())
                    dve.sem_inc(t_dve, 1)
                    dve.reciprocal(s_den, s_den).then_inc(dve_own, 1)
                    dve.wait_ge(dve_own, own.done())
                    dve.sem_inc(t_dve, 1)
                    dve.tensor_tensor(heads_of(pr_s, P), heads_of(pr_s, P), over(s_den, P), ALU.mult).then_inc(p_ok, 1)
                    if j == 3:
                        low(i + (S_GATE + 1))
                    if j % 2 == 0:
                        dve.wait_ge(ot_st, i * 32 + 16 * (j // 2 + 1))
                        dve.sem_inc(t_dve, 1)
                    dve.wait_ge(pv_done, n + 3)
                    dve.sem_inc(t_dve, 1)
                    dve.tensor_copy(oT_s[:, :, (j % 2) * CHUNK:(j % 2 + 1) * CHUNK], heads_of(bank(6), CHUNK)
                                  ).then_inc(ot_ev, 1)
            with dve.Fori(0, 2) as i:
                low(i + (S_KV + 1))
            low(S_LR, P)
            low(S_GQ)
            low(S_R)

            dve.wait_ge(gu_one, 2)
            dve.sem_inc(go_st, 16)
            dve.memset(st_b, 0.0).then_inc(dve_own, 1)
            dve.wait_ge(dve_own, own.done())
            dve.sem_inc(go_ev, 1)

            def log_decays(t, j):
                dve.wait_ge(gg_abs, t + 1)
                dve.sem_inc(t_dve, 1)
                dve.scalar_tensor_tensor(gla_l, bank(0), 0.0, gla_t[j], ALU.min, ALU.subtract).then_inc(gg_la, 1)

            def decayed_keys(t, j):
                dve.wait_ge(gg_dec, t + 1)
                dve.sem_inc(t_dve, 1)
                dve.tensor_tensor(kdec, kvst[j][:, 0:SL], gla_t[j], ALU.mult).then_inc(gg_kd, 1)

            def states(t, j):
                for c, (new, old) in enumerate(((st_a, st_b), (st_b, st_a))):
                    dve.wait_ge(gu_mm, t * 2 + (c + 1))
                    dve.sem_inc(t_dve, 1)
                    for h in range(GH):
                        dve.scalar_tensor_tensor(new[:, h, :], old[:, h, :], gam[j][:, h, c:c + 1],
                                                 bank(2 + 2 * c, 2)[:, h * GV:(h + 1) * GV], ALU.mult, ALU.add
                                                 ).then_inc(gs_up, 1)
                    dve.wait_ge(gs_up, t * 8 + 4 * (c + 1))
                    dve.sem_inc(t_dve, 1)

            def outputs_out(t):
                dve.wait_ge(go_sq, t + 1)
                dve.sem_inc(t_dve, 1)
                dve.tensor_reduce(ssq[:, bass.ds(t, 1), :].rearrange("p a h -> p (a h)"), heads_of(o_q, GV), AX.X, ALU.add)
                dve.wait_ge(go_st, t * 16 + 16)
                dve.sem_inc(t_dve, 1)
                dve.tensor_copy(o_s, bank(6, 2)).then_inc(go_ev, 1)
            log_decays(0, 0)
            decayed_keys(0, 0)
            with dve.Fori(0, NT // 2 - 1) as v:
                for j in range(2):
                    t = v * 2 + j
                    log_decays(t + 1, 1 - j)
                    states(t, j)
                    decayed_keys(t + 1, 1 - j)
                    outputs_out(t)
            log_decays(NT - 1, 1)
            states(NT - 2, 0)
            decayed_keys(NT - 1, 1)
            outputs_out(NT - 2)
            states(NT - 1, 1)
            outputs_out(NT - 1)
            dve.wait_ge(go_ev, NT + 1)
            dve.tensor_scalar(ssq, ssq, 1.0 / GV, EPS, ALU.mult, ALU.add).then_inc(rs_v, 1)
            dve.wait_ge(rs_s, 1)
            dve.reciprocal(ssq, ssq).then_inc(dve_own, 1)
            dve.wait_ge(dve_own, own.done())
            dve.wait_ge(gu_ld, 48)
            for i in range(NS):
                for t in range(NT):
                    if t == NT - 1:
                        low(S_R + 1 + i)
                    j, n = t % 2, i * (NT // 2) + t // 2
                    dve.wait_ge(o_ld[j], 16 * (n + 2))
                    dve.wait_ge(pj_free[j], B_R + n + 2)
                    if n:
                        dve.wait_ge(a_ok[j], n)
                    for h in range(2):
                        dve.scalar_tensor_tensor(rtmp[j][:, h * GV:(h + 1) * GV], opc[j][:, h * GV:(h + 1) * GV],
                                               ssq[:, t, 2 * i + h:2 * i + h + 1],
                                               rsil[j][:, h * GV:(h + 1) * GV], ALU.mult, ALU.mult).then_inc(dve_own, 1)
                        dve.wait_ge(dve_own, own.done())
                    if n:
                        dve.wait_ge(a_st[j], 16 * n)
                    dve.tensor_tensor(apc[j], rtmp[j], ng_bc[:, i * SL:(i + 1) * SL], ALU.mult).then_inc(a_ok[j], 1)
                    if i == NS - 1 and t > 3:
                        for h in range(2):
                            tile_low(t - 4, h, 2 * NT + 2 * (t - 4) + h + 1)
            for t in range(NT - 4, NT):
                for h in range(2):
                    tile_low(t, h, 2 * NT + 2 * t + h + 1)

            for s, base, nb in ((S_WG, 0, B_WG), (S_WS, KC, B_WS)):
                for k in range(KC):
                    for h in range(2):
                        if k % CPS == CPS - 1 and h == 1:
                            low(s + 1 + k // CPS)
                        dve.wait_ge(gt_free[h], base + k + 1)
                        dve.wait_ge(pj_done[h], nb + k + 1)
                        m = mT[:, k, h * SL:(h + 1) * SL]
                        out = mtmp[h] if base else m
                        if base and k:
                            dve.wait_ge(m_ok, 2 * k + h - 1)
                        dve.tensor_tensor(out, bank(h), gsg[h], ALU.mult).then_inc(pj_free[h], 1)
                        if base:
                            dve.wait_ge(pj_free[h], nb + k + 2)
                            dve.tensor_tensor(m, m, mtmp[h], ALU.add).then_inc(m_ok, 1)
                if base == 0:
                    for k in range(KC):
                        dve.wait_ge(tp_hi, 4 * NT + k + 1)
                        dve.tensor_tensor(act_l[:, k, :], bst[k % 4], f(act_h[:, k, :]), ALU.subtract).then_inc(tp_lo, 1)
            for h in range(2):
                for k in range(KC):
                    dve.wait_ge(tp_hi, 4 * NT + KC * (h + 1) + k + 1)
                    dve.tensor_tensor(act_l[:, k, h * SL:(h + 1) * SL], mT[:, k, h * SL:(h + 1) * SL],
                                      f(act_h[:, k, h * SL:(h + 1) * SL]), ALU.subtract).then_inc(tp_lo, 1)

            def gain_x1(t):
                j = t % 2
                dve.wait_ge(xn_ok, t + 1)
                dve.tensor_tensor(xn[j], xn[j], ln_g, ALU.mult).then_inc(dve_own, 1)
                dve.wait_ge(dve_own, own.done())
                if t > 1:
                    dve.wait_ge(tp_done, 4 + 4 * NT + 2 * (t - 1))
                    dve.wait_ge(x1_stored[j], 16 * (t // 2))
                dve.tensor_tensor(nat[j], xn[j], ln_b, ALU.add).then_inc(x1_ready[j], 1)

            for i in range(NS):
                for t in range(NT + 2 * i):
                    if t == NT - 1:
                        low(S_WO + 1 + i, SL if i == 0 else NLOG)
                    j, n = t % 2, i * (NT // 2) + t // 2
                    if t < NT:
                        dve.wait_ge(xp_ld[j], 16 * (n + 1))
                        dve.wait_ge(pj_done[j], B_WO + n + 1)
                        piece = y_n[:, t, i * SL:(i + 1) * SL]
                        dve.scalar_tensor_tensor(piece, xpc[j], ALPHA, bank(j), ALU.mult, ALU.add).then_inc(pj_free[j], 1)
                        dve.wait_ge(pj_free[j], B_WO + n + 2)
                        dve.bn_stats(stats[:, t, i, :], piece).then_inc(dve_own, 1)
                        dve.wait_ge(dve_own, own.done())
                    if i == 0:
                        continue
                    if t < NT:
                        dve.bn_aggr(mv[:, t, :], stats[:, t].rearrange("p i s -> p (i s)")).then_inc(dve_own, 1)
                        dve.wait_ge(dve_own, own.done())
                        dve.tensor_scalar(rstd[:, t:t + 1], mv[:, t, 1:2], EPS, None, ALU.add).then_inc(ln_v, 1)
                    if t == 0:
                        dve.wait_ge(ln_ld, 32)
                    if 0 < t <= NT:
                        gain_x1(t - 1)
                    if t < NT:
                        dve.wait_ge(ln_s, t + 1)
                        dve.reciprocal(rstd[:, t:t + 1], rstd[:, t:t + 1]).then_inc(dve_own, 1)
                        dve.wait_ge(dve_own, own.done())
                        dve.scalar_tensor_tensor(nmr[:, t:t + 1], mv[:, t, 0:1], -1.0, rstd[:, t:t + 1],
                                                 ALU.mult, ALU.mult).then_inc(ln_r, 1)
                    if t > 1:
                        for h in range(2):
                            tile_low(t - 2, h, 4 * NT + 3 * KC + 2 * (t - 2) + h + 1)
            low(S_PG)

            dve.wait_ge(lg_tp, 1)
            dve.wait_ge(pw_ld, 64)
            dve.tensor_tensor(lg, bank(2, 2).rearrange("p (t n) -> p t n", t=NT)[:, :, 0:NLOG],
                            along(rb_bc, NT), ALU.add).then_inc(dve_own, 1)
            dve.wait_ge(dve_own, own.done())
            lg_g = lg[:, :, 0:NG]
            i8 = cst[:, K_I8:K_I8 + EPG]

            def first_of(onehot, x, mx, n, scratch, ix):
                dve.tensor_reduce(mx, x, AX.X, ALU.max).then_inc(dve_own, 1)
                dve.wait_ge(dve_own, own.done())
                dve.tensor_tensor(scratch, x, over(mx, n), ALU.is_ge).then_inc(dve_own, 1)
                dve.wait_ge(dve_own, own.done())
                dve.tensor_tensor(scratch, scratch, along(i8[:, 0:n], NT), ALU.mult).then_inc(dve_own, 1)
                dve.wait_ge(dve_own, own.done())
                dve.tensor_reduce(ix, scratch, AX.X, ALU.min).then_inc(dve_own, 1)
                dve.wait_ge(dve_own, own.done())
                dve.tensor_tensor(onehot, along(i8[:, 0:n], NT), over(ix, n), ALU.is_equal).then_inc(dve_own, 1)
                dve.wait_ge(dve_own, own.done())
            first_of(g_oh, lg_g, g_mx, NG, g_e, g_ix)
            dve.tensor_tensor(g_e, lg_g, over(g_mx, NG), ALU.subtract).then_inc(r_mx, 1)
            e4 = e_all.rearrange("p t (g e) -> p t g e", g=NG)
            for g in range(NG):
                x = lg[:, :, NG + EPG * g:NG + EPG * (g + 1)]
                dve.tensor_tensor(e4[:, :, g, :], x, g_oh[:, :, g:g + 1].to_broadcast([P, NT, EPG]), ALU.mult).then_inc(dve_own, 1)
                dve.wait_ge(dve_own, own.done())
            dve.tensor_tensor(e_sel, e4[:, :, 0, :], e4[:, :, 1, :], ALU.add).then_inc(dve_own, 1)
            dve.wait_ge(dve_own, own.done())
            for g in range(2, NG):
                dve.tensor_tensor(e_sel, e_sel, e4[:, :, g, :], ALU.add).then_inc(dve_own, 1)
                dve.wait_ge(dve_own, own.done())
            first_of(e_oh[0], e_sel, e_mx[0], EPG, e_t, g_ix)
            dve.scalar_tensor_tensor(e_m, e_oh[0], NEG, e_sel, ALU.mult, ALU.add).then_inc(dve_own, 1)
            dve.wait_ge(dve_own, own.done())
            first_of(e_oh[1], e_m, e_mx[1], EPG, e_t, g_ix)
            dve.tensor_tensor(e_mx[1], e_mx[1], e_mx[0], ALU.subtract).then_inc(r_dif, 1)
            for c in range(2):
                o4 = oh[c].rearrange("p t (g e) -> p t g e", g=NG)
                for g in range(NG):
                    dve.tensor_tensor(o4[:, :, g, :], e_oh[c], g_oh[:, :, g:g + 1].to_broadcast([P, NT, EPG]),
                                    ALU.mult).then_inc(dve_own, 1)
                    dve.wait_ge(dve_own, own.done())
            dve.tensor_tensor(ohs, oh[0], oh[1], ALU.add).then_inc(r_oh, 1)
            dve.wait_ge(r_ex, 1)
            dve.tensor_reduce(g_sum, g_e, AX.X, ALU.add).then_inc(dve_own, 1)
            dve.wait_ge(dve_own, own.done())
            dve.wait_ge(r_e2, 1)
            dve.tensor_scalar(e_mx[0], e_mx[1], 1.0, None, ALU.add).then_inc(dve_own, 1)
            dve.wait_ge(dve_own, own.done())
            dve.tensor_tensor(e_mx[0], e_mx[0], g_sum, ALU.mult).then_inc(dve_own, 1)
            dve.wait_ge(dve_own, own.done())
            dve.reciprocal(slot_w[:, 0, :], e_mx[0]).then_inc(dve_own, 1)
            dve.wait_ge(dve_own, own.done())
            dve.tensor_tensor(slot_w[:, 1, :], slot_w[:, 0, :], e_mx[1], ALU.mult).then_inc(dve_own, 1)
            dve.wait_ge(dve_own, own.done())

            def place():
                dve.wait_ge(r_mm, 1)
                earlier = bank(6)[:, 0:NT * NE].rearrange("p (t e) -> p t e", t=NT)
                in_tile = bank(7)[:, 0:NT * NE].rearrange("p (t e) -> p t e", t=NT)
                dve.memset(pre[:, 0, :], 0.0).then_inc(dve_own, 1)
                dve.wait_ge(dve_own, own.done())
                for t in range(1, NT):
                    dve.tensor_tensor(pre[:, t, :], pre[:, t - 1, :], in_tile[:, t - 1, :], ALU.add).then_inc(dve_own, 1)
                    dve.wait_ge(dve_own, own.done())
                dve.tensor_tensor(cnt, pre[:, NT - 1, :], in_tile[:, NT - 1, :], ALU.add).then_inc(dve_own, 1)
                dve.wait_ge(dve_own, own.done())
                dve.tensor_tensor(rank, pre, earlier, ALU.add).then_inc(dve_own, 1)
                dve.wait_ge(dve_own, own.done())
                dve.tensor_scalar(nbk, cnt, 0.0, None, ALU.is_gt).then_inc(dve_own, 1)
                dve.wait_ge(dve_own, own.done())
                for m in range(1, SEQ // P):
                    dve.scalar_tensor_tensor(nbk, cnt, float(P * m), nbk, ALU.is_gt, ALU.add).then_inc(dve_own, 1)
                    dve.wait_ge(dve_own, own.done())
                x, y = btmp, bend
                dve.tensor_copy(x, nbk).then_inc(dve_own, 1)
                dve.wait_ge(dve_own, own.done())
                for sh in (1, 2, 4, 8, 16):
                    dve.tensor_copy(y[:, 0:sh], x[:, 0:sh]).then_inc(dve_own, 1)
                    dve.wait_ge(dve_own, own.done())
                    dve.tensor_tensor(y[:, sh:NE], x[:, sh:NE], x[:, 0:NE - sh], ALU.add).then_inc(dve_own, 1)
                    dve.wait_ge(dve_own, own.done())
                    x, y = y, x
                dve.tensor_tensor(nbk, x, nbk, ALU.subtract).then_inc(dve_own, 1)
                dve.wait_ge(dve_own, own.done())
                dve.tensor_scalar(nbk, nbk, float(P), None, ALU.mult).then_inc(dve_own, 1)
                dve.wait_ge(dve_own, own.done())
                dve.tensor_tensor(rank, rank, along(nbk, NT), ALU.add).then_inc(dve_own, 1)
                dve.wait_ge(dve_own, own.done())
                for c in range(2):
                    dve.tensor_tensor(rt, oh[c], rank, ALU.mult).then_inc(dve_own, 1)
                    dve.wait_ge(dve_own, own.done())
                    dve.tensor_reduce(slot_f, rt, AX.X, ALU.add).then_inc(dve_own, 1)
                    dve.wait_ge(dve_own, own.done())
                    dve.tensor_copy(slot_i[:, c, :], slot_f).then_inc(slots_ok, 1)
                dve.tensor_scalar(nb_i, x[:, NE - 1:NE], float(-MINB), None, ALU.add).then_inc(dve_own, 1)
                dve.wait_ge(dve_own, own.done())
                dve.tensor_tensor(be_cmp, along(x[0:1, :], MAXB), over(cst[0:1, K_I48:K_I48 + MAXB], NE), ALU.is_le).then_inc(dve_own, 1)
                dve.wait_ge(dve_own, own.done())
                dve.tensor_reduce(be_f, be_cmp, AX.X, ALU.add).then_inc(dve_own, 1)
                dve.wait_ge(dve_own, own.done())
                dve.tensor_copy(be_row, be_f).then_inc(nb_ok, 1)

            for i in range(NS):
                for t in range(NT):
                    j, n = t % 2, i * (NT // 2) + t // 2
                    dve.wait_ge(pj_done[j], B_PG + n + 1)
                    dve.tensor_tensor(gpre[j], bank(j), pg_bc[:, i * SL:(i + 1) * SL], ALU.add).then_inc(pj_free[j], 1)
                    if i == 0 and t == NT - 1:
                        low(S_PG + 1)
                    dve.wait_ge(gs_ok[j], n + 1)
                    dve.wait_ge(pp_done[j], n + 1)
                    if n:
                        dve.wait_ge(z2_ok[j], n)
                    dve.tensor_tensor(ptmp[j], bank(4 + j), gpre[j], ALU.mult).then_inc(pp_free[j], 1)
                    dve.wait_ge(pp_free[j], n + 2)
                    dve.wait_ge(xp_ld[j], 16 * (NT + n + 1))
                    if n:
                        dve.wait_ge(z2_st[j], 16 * n)
                    dve.scalar_tensor_tensor(z2p[j], x1p[j], ALPHA, ptmp[j], ALU.mult, ALU.add).then_inc(z2_ok[j], 1)
                    if (i, t) == (0, 2):
                        place()

            dve.wait_ge(nb_ok, 1)
            last_b = dve.snap(dve.value_load(nb_i[0:1, 0:1], min_val=0, max_val=MAXB - MINB) + (MINB - 1))

            def low_expert(m, b, dst, high, src):
                w = dst.shape[1] // WC
                for c in range(WC):
                    dve.wait_ge(m_hi[m], b * WC + (c + 1))
                    dve.sem_inc(t_dve, 1)
                    dve.tensor_tensor(dst[:, w * c:w * (c + 1), :], arrived(src, m, b, slice(w * c, w * (c + 1))),
                                    f(high[:, w * c:w * (c + 1), :]), ALU.subtract).then_inc(m_lo[m], 1)

            def x_low(b):
                for h in range(2):
                    dve.wait_ge(xt_hi, b * 2 + (h + 1))
                    dve.sem_inc(t_dve, 1)
                    dve.tensor_tensor(blk_l[:, 4 * h:4 * h + 4, :], bank(2 + h).rearrange("p (k n) -> p k n", k=4),
                                    f(blk_h[:, 4 * h:4 * h + 4, :]), ALU.subtract).then_inc(xt_lo, 1)

            def hidden(b, first):
                dve.wait_ge(sl_ok, b + 1)
                dve.sem_inc(t_dve, 1)
                dve.wait_ge(um_done, b + 1)
                dve.sem_inc(t_dve, 1)
                if not first:
                    dve.wait_ge(ht_done, b)
                    dve.sem_inc(t_dve, 1)
                dve.tensor_tensor(hid, bank(1), sig, ALU.mult).then_inc(h_ok, 1)

            def block_step(b, first, last):
                if first:
                    hidden(b, True)
                    low_expert(2, b, d_l, d_h, ring_down)
                if not last:
                    low_expert(0, b + 1, wgt_l, wgt_h, ring_up)
                    low_expert(1, b + 1, u_l, u_h, ring_up)
                if not first:
                    hidden(b, False)
                if not last:
                    x_low(b + 1)
                if not first:
                    low_expert(2, b, d_l, d_h, ring_down)
                dve.wait_ge(ht_hi, b + 1)
                dve.sem_inc(t_dve, 1)
                dve.tensor_tensor(blk_l[:, KC:KC + FC, :], bank(4).rearrange("p (k n) -> p k n", k=FC),
                                  f(blk_h[:, KC:KC + FC, :]), ALU.subtract).then_inc(ht_lo, 1)
            low_expert(0, 0, wgt_l, wgt_h, ring_up)
            x_low(0)
            low_expert(1, 0, u_l, u_h, ring_up)
            block_step(0, True, False)
            with dve.Fori(1, last_b) as b:
                block_step(b, False, False)
            block_step(last_b, False, True)

            dve.wait_ge(z_ld, 16 * NT)
            for t in range(NT):
                j = t % 2
                dve.wait_ge(f_z[t % (NT // 2)], 32 * (t // (NT // 2) + 1))
                for c, y in enumerate((y0, y1)):
                    dve.scalar_tensor_tensor(zt[t], y[t % (NT // 2)], slot_w[:, c, t:t + 1], zt[t],
                                             ALU.mult, ALU.add).then_inc(dve_own, 1)
                    dve.wait_ge(dve_own, own.done())
                for i in range(NS):
                    dve.bn_stats(fst[:, j, i, :], zt[t][:, i * SL:(i + 1) * SL]).then_inc(dve_own, 1)
                    dve.wait_ge(dve_own, own.done())
                dve.bn_aggr(fmv[:, j, :], fst[:, j].rearrange("p i s -> p (i s)")).then_inc(dve_own, 1)
                dve.wait_ge(dve_own, own.done())
                if t > 1:
                    dve.wait_ge(f_n, t - 1)
                dve.tensor_scalar(frs[:, j, :], fmv[:, j, 1:2], EPS, None, ALU.add).then_inc(f_var, 1)
                dve.wait_ge(f_sq, t + 1)
                dve.reciprocal(frs[:, j, :], frs[:, j, :]).then_inc(dve_own, 1)
                dve.wait_ge(dve_own, own.done())
                dve.scalar_tensor_tensor(fnm[:, j, :], fmv[:, j, 0:1], -1.0, frs[:, j, :], ALU.mult, ALU.mult
                                         ).then_inc(f_rs, 1)


_INS = ["x", "p", "rel_table", "w_in", "gla_gate_up", "gla_gate_b", "gla_norm_g", "swa_sinks",
        "branch_gate_b", "w_branch_gla", "w_branch_swa", "w_out", "ln1_g", "ln1_b",
        "router_group_w", "router_group_b", "router_expert_w", "router_expert_b",
        "expert_w_gate", "expert_w_up", "expert_w_down", "w_ple", "w_ple_gate", "ple_gate_b",
        "ln2_g", "ln2_b"]


def shape_constants():
    i = np.arange(P)
    cst = np.zeros((P, K_ALL), np.float32)
    cst[:, K_ID:K_ID + P] = np.eye(P)
    cst[:, K_SUF:K_SUF + P] = (i[:, None] > i[None, :]) & (i[:, None] // CHUNK == i[None, :] // CHUNK)
    cst[:, K_ERL:K_ERL + P] = i[:, None] < i[None, :]
    cst[:, K_ONE:K_ONE + P] = 1
    cst[:, K_CH:K_CH + 2] = i[:, None] // CHUNK == np.arange(2)[None, :]
    cst[:, K_I8:K_I8 + EPG] = np.arange(EPG) - EPG
    cst[:, K_I48:K_I48 + MAXB] = np.arange(MAXB)
    tok = i[:, None] + P * np.arange(NT)[None, :]
    toki = np.stack([np.stack([tok, c * SEQ + tok], -1) for c in range(2)], 1).astype(np.int32)
    s = np.arange(MAXB * P)
    empty = np.stack([0 * s, 2 * SEQ + s % P], 1).astype(np.int32)
    rel = np.arange(REL) - (P - 1)
    half, exact = 16, 8
    n = np.abs(rel)
    large = exact + (np.log(np.maximum(n, 1) / exact) / np.log(128 / exact) * (half - exact)).astype(np.int32)
    b = (rel > 0) * half + np.where(n < exact, n, np.minimum(large, half - 1))
    bucket = (np.arange(2 * half)[:, None] == b[None, :]).astype(np.float32)
    return {"cst": cst, "toki": toki, "bucket": bucket, "empty": empty}


def kernel(**inputs):
    import concourse.bacc as _bacc
    from concourse.bass_utils import run_bass_kernel_spmd as _run

    nc = _bacc.Bacc("TRN2", target_bir_lowering=False, num_devices=1)
    given = {k: np.ascontiguousarray(inputs[k]) for k in _INS}
    given.update(shape_constants())
    a = {k: nc.dram_tensor(f"in_{k}", v.shape, mybir.dt.from_np(v.dtype), kind="ExternalInput").ap()
         for k, v in given.items()}
    a["out"] = nc.dram_tensor("out_0", (1, SEQ, D), F32, kind="ExternalOutput").ap()
    build(nc, a)
    r = _run(nc, [{f"in_{k}": v for k, v in given.items()}], core_ids=[0])
    return r.results[0]["out_0"]
```
